# Optimizing a Trainium2 kernel written in Bass

```python
import jax
import jax.numpy as jnp
from jax import lax
import numpy as np

D_MODEL = 2048
BATCH = 1
SEQ = 256
DEPTH = 2

RET_HEAD_DIM = 256
RET_HEADS = (D_MODEL // 2) // RET_HEAD_DIM
RET_WIDTH = RET_HEADS * RET_HEAD_DIM
RET_CHUNK = 128
POOL_WINDOWS = (2, 4, 8, 16)
POOL_WIDTH = D_MODEL - RET_WIDTH
POOL_GROUP = POOL_WIDTH // len(POOL_WINDOWS)
EVEN_IN = 4 * RET_WIDTH + POOL_WIDTH
ATTN_HEAD_DIM = 64
ATTN_Q_HEADS = D_MODEL // ATTN_HEAD_DIM
ATTN_KV_HEADS = ATTN_Q_HEADS // 8
ATTN_GROUP = ATTN_Q_HEADS // ATTN_KV_HEADS
ATTN_Q_WIDTH = ATTN_Q_HEADS * ATTN_HEAD_DIM
ATTN_KV_WIDTH = ATTN_KV_HEADS * ATTN_HEAD_DIM
ODD_IN = ATTN_Q_WIDTH + 2 * ATTN_KV_WIDTH
WINDOW = 128
ATTN_BLOCK = 128
D_FF = 5632
CONV_WIDTH = 3
N_EVEN = (DEPTH + 1) // 2
N_ODD = DEPTH // 2
DEEPNORM_ALPHA = (2 * DEPTH) ** 0.25
DEEPNORM_BETA = (8 * DEPTH) ** -0.25
LN_EPS = 1e-5

kernel_name = 'hybrid_retention_pool_swa_sink_convffn'

def layer_norm(x, g, b):
    xf = x.astype(jnp.float32)
    mu = jnp.mean(xf, axis=-1, keepdims=True)
    var = jnp.mean(jnp.square(xf - mu), axis=-1, keepdims=True)
    return ((xf - mu) * lax.rsqrt(var + LN_EPS) * g + b).astype(x.dtype)

def head_norm(y):
    mu = jnp.mean(y, axis=-1, keepdims=True)
    var = jnp.mean(jnp.square(y - mu), axis=-1, keepdims=True)
    return (y - mu) * lax.rsqrt(var + LN_EPS)

def retention_chunkwise(q, k, v):
    B, S, H, dk = q.shape
    C = RET_CHUNK
    N = S // C
    log_gamma = jnp.log1p(-(2.0 ** (-5.0 - jnp.arange(H, dtype=jnp.float32))))
    qc = q.reshape(B, N, C, H, dk)
    kc = (k * dk ** -0.5).reshape(B, N, C, H, dk)
    vc = v.reshape(B, N, C, H, v.shape[-1])
    pos = jnp.arange(C, dtype=jnp.float32)
    diff = pos[:, None] - pos[None, :]
    decay_in = jnp.where(diff[None] >= 0,
                         jnp.exp(log_gamma[:, None, None] * jnp.maximum(diff, 0.0)[None]), 0.0)
    scores = jnp.einsum('bnihd,bnjhd->bnhij', qc, kc) * decay_in
    inner = jnp.einsum('bnhij,bnjhe->bnihe', scores, vc)
    zeta = jnp.exp(log_gamma[:, None] * (C - 1.0 - pos)[None, :])
    kv = jnp.einsum('bnjhd,hj,bnjhe->bnhde', kc, zeta, vc)
    chunk_decay = jnp.exp(log_gamma * C)[:, None, None]

    def step(state, kv_n):
        return state * chunk_decay + kv_n, state

    init = jnp.zeros((B, H, dk, vc.shape[-1]), jnp.float32)
    _, prev = lax.scan(step, init, jnp.moveaxis(kv, 1, 0))
    prev = jnp.moveaxis(prev, 0, 1)
    xi = jnp.exp(log_gamma[:, None] * (pos + 1.0)[None, :])
    cross = jnp.einsum('bnihd,bnhde,hi->bnihe', qc, prev, xi)
    return (inner + cross).reshape(B, S, H, vc.shape[-1])

def multiscale_pool(u, pool_w, pool_scale):
    B, S, _ = u.shape
    uf = u.astype(jnp.float32)
    cs = jnp.cumsum(uf, axis=1)
    t = jnp.arange(S)
    outs = []
    for gi, w in enumerate(POOL_WINDOWS):
        lo, hi = gi * POOL_GROUP, (gi + 1) * POOL_GROUP
        csg = cs[..., lo:hi]
        lagged = jnp.pad(csg, ((0, 0), (w, 0), (0, 0)))[:, :S]
        count = jnp.minimum(t + 1, w).astype(jnp.float32)[None, :, None]
        pooled = (csg - lagged) / count - uf[..., lo:hi]
        outs.append(pooled @ pool_w[gi].astype(jnp.float32))
    return (jnp.concatenate(outs, axis=-1) * pool_scale.astype(jnp.float32)).astype(u.dtype)

def retention_pool_mixer(x, w_in, pool_w, pool_scale, w_out):
    B, S, _ = x.shape
    h = x @ w_in
    q, k, v, g, u = jnp.split(h, [RET_WIDTH, 2 * RET_WIDTH, 3 * RET_WIDTH, 4 * RET_WIDTH], axis=-1)
    heads = lambda a: a.astype(jnp.float32).reshape(B, S, RET_HEADS, RET_HEAD_DIM)
    y = head_norm(retention_chunkwise(heads(q), heads(k), heads(v))).reshape(B, S, RET_WIDTH)
    y_ret = (jax.nn.silu(g.astype(jnp.float32)) * y).astype(x.dtype)
    y_pool = multiscale_pool(u, pool_w, pool_scale)
    return jnp.concatenate([y_ret, y_pool], axis=-1) @ w_out

def alibi_slopes(n):
    start = 2.0 ** (-8.0 / n)
    return start ** jnp.arange(1, n + 1, dtype=jnp.float32)

def with_prev_block(a):
    pad = [(0, 0), (1, 0)] + [(0, 0)] * (a.ndim - 2)
    prev = jnp.pad(a[:, :-1], pad)
    return jnp.concatenate([prev, a], axis=2)

def swa_sink_attention(x, w_qkv, b_qkv, sinks, w_out):
    B, S, _ = x.shape
    L = ATTN_BLOCK
    NB = S // L
    h = x @ w_qkv + b_qkv
    q, k, v = jnp.split(h, [ATTN_Q_WIDTH, ATTN_Q_WIDTH + ATTN_KV_WIDTH], axis=-1)
    q = q.reshape(B, NB, L, ATTN_KV_HEADS, ATTN_GROUP, ATTN_HEAD_DIM)
    kb = with_prev_block(k.reshape(B, NB, L, ATTN_KV_HEADS, ATTN_HEAD_DIM))
    vb = with_prev_block(v.reshape(B, NB, L, ATTN_KV_HEADS, ATTN_HEAD_DIM))
    scores = jnp.einsum('bnikgd,bnjkd->bnkgij', q, kb).astype(jnp.float32) * ATTN_HEAD_DIM ** -0.5
    i = jnp.arange(L)
    j = jnp.arange(2 * L)
    delta = L + i[:, None] - j[None, :]
    s_pos = jnp.arange(NB)[:, None] * L - L + j[None, :]
    valid = (delta >= 0)[None] & (delta < WINDOW)[None] & (s_pos >= 0)[:, None, :]
    slopes = alibi_slopes(ATTN_Q_HEADS).reshape(ATTN_KV_HEADS, ATTN_GROUP)
    bias = -slopes[:, :, None, None] * delta.astype(jnp.float32)
    scores = jnp.where(valid[None, :, None, None], scores + bias[None, None], -jnp.inf)
    sink = sinks.astype(jnp.float32).reshape(ATTN_KV_HEADS, ATTN_GROUP)[None, None, :, :, None, None]
    m = jnp.maximum(jnp.max(scores, axis=-1, keepdims=True), sink)
    p = jnp.exp(scores - m)
    probs = p / (jnp.sum(p, axis=-1, keepdims=True) + jnp.exp(sink - m))
    o = jnp.einsum('bnkgij,bnjkd->bnikgd', probs.astype(vb.dtype), vb)
    return o.reshape(B, S, ATTN_Q_WIDTH) @ w_out

def conv_glu_ffn(x, w_in, conv_w, conv_b, w_out):
    S = x.shape[1]
    h = x @ w_in
    hp = jnp.pad(h, ((0, 0), (CONV_WIDTH - 1, 0), (0, 0)))
    hc = conv_b + hp[:, 0:S] * conv_w[0]
    for kk in range(1, CONV_WIDTH):
        hc = hc + hp[:, kk:kk + S] * conv_w[kk]
    gate, val = jnp.split(hc, 2, axis=-1)
    return (jax.nn.gelu(gate, approximate=False) * val) @ w_out

def setup_inputs(seed: int = 0) -> dict:
    key = jax.random.key(seed)
    ks = jax.random.split(key, 16)

    def nrm(k, shape, scale):
        return jax.random.normal(k, shape, jnp.float32) * scale

    return {
        'x': nrm(ks[0], (BATCH, SEQ, D_MODEL), 1.0),
        'ln_gain': 1.0 + nrm(ks[1], (DEPTH, 2, D_MODEL), 0.02),
        'ln_bias': nrm(ks[2], (DEPTH, 2, D_MODEL), 0.02),
        'even_w_in': nrm(ks[3], (N_EVEN, D_MODEL, EVEN_IN), D_MODEL ** -0.5),
        'pool_w': nrm(ks[4], (N_EVEN, len(POOL_WINDOWS), POOL_GROUP, POOL_GROUP), POOL_GROUP ** -0.5),
        'pool_scale': 1.0 + nrm(ks[5], (N_EVEN, POOL_WIDTH), 0.1),
        'even_w_out': nrm(ks[6], (N_EVEN, D_MODEL, D_MODEL), DEEPNORM_BETA * D_MODEL ** -0.5),
        'attn_w_qkv': nrm(ks[7], (N_ODD, D_MODEL, ODD_IN), D_MODEL ** -0.5),
        'attn_b_qkv': nrm(ks[8], (N_ODD, ODD_IN), 0.02),
        'attn_sinks': nrm(ks[9], (N_ODD, ATTN_Q_HEADS), 0.5),
        'attn_w_out': nrm(ks[10], (N_ODD, ATTN_Q_WIDTH, D_MODEL), DEEPNORM_BETA * ATTN_Q_WIDTH ** -0.5),
        'ffn_w_in': nrm(ks[11], (DEPTH, D_MODEL, 2 * D_FF), D_MODEL ** -0.5),
        'ffn_conv_w': nrm(ks[12], (DEPTH, CONV_WIDTH, 2 * D_FF), CONV_WIDTH ** -0.5),
        'ffn_conv_b': nrm(ks[13], (DEPTH, 2 * D_FF), 0.02),
        'ffn_w_out': nrm(ks[14], (DEPTH, D_FF, D_MODEL), DEEPNORM_BETA * D_FF ** -0.5),
    }

def reference(x, ln_gain, ln_bias, even_w_in, pool_w, pool_scale, even_w_out,
              attn_w_qkv, attn_b_qkv, attn_sinks, attn_w_out,
              ffn_w_in, ffn_conv_w, ffn_conv_b, ffn_w_out):
    for layer in range(DEPTH):
        li = layer // 2
        if layer % 2 == 0:
            mix = retention_pool_mixer(x, even_w_in[li], pool_w[li], pool_scale[li], even_w_out[li])
        else:
            mix = swa_sink_attention(x, attn_w_qkv[li], attn_b_qkv[li], attn_sinks[li], attn_w_out[li])
        x = layer_norm(DEEPNORM_ALPHA * x + mix, ln_gain[layer, 0], ln_bias[layer, 0])
        ffn = conv_glu_ffn(x, ffn_w_in[layer], ffn_conv_w[layer], ffn_conv_b[layer], ffn_w_out[layer])
        x = layer_norm(DEEPNORM_ALPHA * x + ffn, ln_gain[layer, 1], ln_bias[layer, 1])
    return x


_drawn_inputs = setup_inputs


def setup_inputs(seed=0):
    import zlib

    import numpy as np

    out = dict(_drawn_inputs(seed))
    spreads = {}
    factors = {'attn_b_qkv': 8.0, 'attn_sinks': 5.103, 'ffn_conv_b': 6.075}
    for name, (base, spread) in spreads.items():
        noise = np.random.default_rng([zlib.crc32(name.encode()), seed]).standard_normal(out[name].shape)
        drawn = base * np.exp(spread * noise) if base else spread * noise
        out[name] = jnp.asarray(drawn.astype(out[name].dtype))
    for name, factor in factors.items():
        out[name] = (out[name] * factor).astype(out[name].dtype)
    return out
```

```python
from contextlib import ExitStack

import numpy as np

import concourse.bass as bass
from concourse import mybir

F32 = mybir.dt.float32
F32R = mybir.dt.float32r
ALU = mybir.AluOpType
ACT = mybir.ActivationFunctionType
AX_X = mybir.AxisListType.X

P = 128
SEQ, D = 256, 2048
TOK = SEQ // P
KT = D // P
COLS = 512
GK = 4
KG = KT // GK
NCH = D // COLS
D_FF = 5632
FC = D_FF // COLS
FT = 2 * D_FF // P
TPC = COLS // P
CONV = 3
ALPHA = 4 ** 0.25
EPS = 1e-5
RH, RD = 4, 256
RW = RH * RD
WINDOWS = (2, 4, 8, 16)
AH, AD, KVH = 32, 64, 4
PAIRS = AH // 2
MASKED = -1e37
ARENA = 14080

RAW, HI, LO = 4, 4, 3
HI_LEAD, LO_LEAD = 3, 2

EVEN_COLS = [0, 512, 1024, 1536, 2048, 2560, 4096, 4608, 3072, 3584]
EVEN_OUT_KG = [2, 3, 0, 1]
ODD_COLS = [2048, 0, 512, 1024, 1536]
ODD_OUT_ORDER = [(0, 0), (0, 1), (1, 0), (1, 1), (0, 2), (1, 2), (0, 3), (1, 3)] + \
                [(n, kg) for n in (2, 3) for kg in range(KG)]
S_EVEN_IN = 0
S_EVEN_OUT = S_EVEN_IN + len(EVEN_COLS) * KG
S_FFN0 = S_EVEN_OUT + NCH * KG
FFN_GROUPS = 3 * KG * FC
S_ODD_IN = S_FFN0 + FFN_GROUPS
S_ODD_OUT = S_ODD_IN + len(ODD_COLS) * KG
S_FFN1 = S_ODD_OUT + NCH * KG
S_END = S_FFN1 + FFN_GROUPS
S_FFN = [S_FFN0, S_FFN1]
S_OUT = [S_EVEN_OUT, S_ODD_OUT]

FILL_X, FILL_RET, FILL_LN0, FILL_LN1, FILL_ATT, FILL_LN2 = 0, 8, 12, 20, 28, 36
FILL_LN = [FILL_LN0, FILL_LN1, FILL_LN2]
ATT_FILL_BANKS = [2, 3, 2, 3, 4, 5, 4, 5]


def fill_bank(n):
    if FILL_ATT <= n < FILL_LN2:
        return ATT_FILL_BANKS[n - FILL_ATT]
    return 4 + n % 4


TP_EVEN = 0
TP_FFN0 = TP_EVEN + 8
TP_ODD = TP_FFN0 + 4 * FC
TP_FFN1 = TP_ODD + 1 + KT // 2
TP_FFN = [TP_FFN0, TP_FFN1]

RET_AT = 24
POOL_AT = 32
ATT_AT = S_ODD_IN + 2 * KG
BURSTS = PAIRS + 2
LOOP_OWN = 12


class Count:

    def __init__(self):
        self.n, self.turn, self.per, self.start = 0, None, 0, 0

    def now(self):
        return self.n if self.turn is None else self.n + self.turn * self.per

    def enter(self, turn, per):
        self.turn, self.per, self.start = turn, per, self.n

    def leave(self, turns):
        assert self.n - self.start == self.per, (self.n - self.start, self.per)
        self.n, self.turn = self.start + self.per * turns, None


def build_trunk(nc, x, ln_gain, ln_bias, even_w_in, pool_w, pool_scale, even_w_out, attn_w_qkv, attn_b_qkv,
                attn_sinks, attn_w_out, ffn_w_in, ffn_conv_w, ffn_conv_b, ffn_w_out,
                decay, pool_taps, distance, out):
    tiled = lambda w: w.rearrange("(t p) n -> p t n", p=P)
    w_even_in, w_even_out = tiled(even_w_in[0]), tiled(even_w_out[0])
    w_qkv, w_att_out = tiled(attn_w_qkv[0]), tiled(attn_w_out[0])
    w_ffn_in = [tiled(ffn_w_in[l]) for l in range(2)]
    w_ffn_out = [tiled(ffn_w_out[l]) for l in range(2)]
    x_t = x[0].rearrange("(a p) d -> p a d", p=P)
    out_t = out[0].rearrange("(a p) d -> p a d", p=P)

    with ExitStack() as ctx:
        sb = lambda name, shape, dt=F32: ctx.enter_context(nc.sbuf_tensor(name, shape, dt))
        sem = lambda name: ctx.enter_context(nc.semaphore(name))

        xres = sb("xres", [P, TOK, D])
        T = sb("T", [P, KT, 2 * SEQ], F32R)
        raw = sb("raw", [P, RAW, GK, COLS])
        w_hi = sb("w_hi", [P, HI, GK, COLS], F32R)
        w_lo = sb("w_lo", [P, LO, GK, COLS], F32R)
        gT = sb("gT", [P, TPC, 2 * SEQ], F32R)
        ident = sb("ident", [P, P])
        taps = sb("taps", [P, 8, FT])
        qk_bias = sb("qk_bias", [P, 18])
        p_scale = sb("p_scale", [P, 8])
        stats = sb("stats", [P, TOK, NCH, 6])
        mean_var = sb("mean_var", [P, TOK, 2])
        rstd = sb("rstd", [P, TOK])
        arena = sb("arena", [P, ARENA])

        used_words = [0]

        def take(*shape):
            n = int(np.prod(shape))
            a = arena[:, used_words[0]:used_words[0] + n]
            used_words[0] += n
            assert used_words[0] <= ARENA, used_words[0]
            names = "abcd"[:len(shape)]
            if len(shape) > 1:
                a = a.rearrange(f"p ({' '.join(names)}) -> p {' '.join(names)}",
                                **{c: s for c, s in zip(names, shape)})
            return a

        qT = take(8, SEQ)
        kT = take(8, SEQ)
        v_nat = take(TOK, RW)
        u_nat = take(TOK, RW)
        y_nat = take(TOK, RW)
        rows = y_nat[:, 0].rearrange("p (t n) -> p t n", n=P)
        prow, prow2 = rows[0:FT], y_nat[0:18, 1].rearrange("p (t n) -> p t n", n=P)
        probs = take(2, 3 * P)
        dec = take(RH, 3 * P)
        tapsw = take(4, 3 * P)
        pw = sb("pw", [P, 4, 2, 256])
        pooledT = qT
        poolT = kT
        silu_g = v_nat
        r_stats = sb("r_stats", [P, TOK * RH, 6])
        r_mv = sb("r_mv", [P, TOK * RH, 2])
        r_std = sb("r_std", [P, TOK * RH, 1])
        used_words[0] = 0
        aqT = take(KT, SEQ)
        akT = take(KVH, SEQ)
        o_nat = take(TOK, D)
        av = take(TOK, KVH * AD)
        S = take(2, 3 * P)
        PT = take(2, 3 * P)
        dist = take(3 * P)
        v_bias = take(KVH * AD)
        m_pair, nm, es, rs, rinv = (sb(f"att{i}", [P, PAIRS, 2, 2]) for i in range(5))
        neg_sink = sb("neg_sink", [P, AH, 2])
        sink_row = sb("sink_row", [P, AH])
        used_words[0] = 0
        lnp = take(2, D)
        half = sb("half", [P, 2, 2, SEQ])
        h = take(TPC, CONV - 1 + SEQ)
        conv_g = take(TPC, SEQ)
        conv_v = take(TPC, SEQ)
        gated = take(TPC, SEQ)
        cur = sb("cur", [P, 2, 4, TPC])

        ps = ctx.enter_context(nc.psum_tensor("ps", [P, 8, COLS], F32))

        raw_landed = [sem(f"raw_landed{i}") for i in range(RAW)]
        x_landed = [sem(f"x_landed{i}") for i in range(NCH)]
        const_landed = sem("const_landed")
        lnp_landed = sem("lnp_landed")
        stored = sem("stored")
        key_copied = sem("key_copied")
        ident_ready = sem("ident_ready")
        scaled = sem("scaled")
        hi_ready = sem("hi_ready")
        lo_ready = sem("lo_ready")
        used = sem("used")
        turned = sem("turned")
        t_hi = sem("t_hi")
        t_ready = sem("t_ready")
        params_turned = sem("params_turned")
        params_ready = sem("params_ready")
        half_out = sem("half_out")
        added = sem("added")
        vug_out = sem("vug_out")
        ret_scored = sem("ret_scored")
        ret_probs = sem("ret_probs")
        ret_mixed = sem("ret_mixed")
        ret_out = sem("ret_out")
        ret_gated = sem("ret_gated")
        pooled = sem("pooled")
        pooled_out = sem("pooled_out")
        pool_mixed = sem("pool_mixed")
        pool_out = sem("pool_out")
        pool_hi = sem("pool_hi")
        pool_ready = sem("pool_ready")
        proj_added = sem("proj_added")
        var_ready = sem("var_ready")
        std_ready = sem("std_ready")
        ln_chunk = sem("ln_chunk")
        conv_done = sem("conv_done")
        gelu_out = sem("gelu_out")
        gated_out = sem("gated_out")
        g_hi = sem("g_hi")
        g_ready = sem("g_ready")
        ffn_added = sem("ffn_added")
        akv_ready = sem("akv_ready")
        att_scored = sem("att_scored")
        att_biased = sem("att_biased")
        att_max = sem("att_max")
        att_exp = sem("att_exp")
        att_turned = sem("att_turned")
        att_pt = sem("att_pt")
        att_mixed = sem("att_mixed")
        att_out = sem("att_out")
        dve_step = sem("dve_step")

        block = ctx.enter_context(nc.Block())

        ret_bank = lambda hd: 4 + hd % 2
        mix_bank = lambda hd: 6 + hd % 2

        @block.sync
        def _(sp):
            def load(s, source, turn=0):
                if not isinstance(turn, int) or s >= RAW:
                    sp.wait_ge(lo_ready, s - RAW + 1 + turn * 12)
                sp.dma_start(raw[:, s % RAW], source).then_inc(raw_landed[s % RAW], 16)

            def load_params(m):
                l, which = divmod(m, 2)
                sp.dma_start(lnp[:, 0], ln_gain[l, which:which + 1, :].to_broadcast([P, D])) \
                    .then_inc(lnp_landed, 16)
                sp.dma_start(lnp[:, 1], ln_bias[l, which:which + 1, :].to_broadcast([P, D])) \
                    .then_inc(lnp_landed, 16)

            def cols(c, n=COLS):
                return slice(c, c + n)

            def even_in(s):
                c, kg = divmod(s - S_EVEN_IN, KG)
                load(s, w_even_in[:, GK * kg:GK * kg + GK, cols(EVEN_COLS[c])])

            def hidden(l, s, c, value, turn=0):
                for kg in range(KG):
                    load(s + kg, w_ffn_in[l][:, GK * kg:GK * kg + GK, bass.ds(c * COLS + value * D_FF, COLS)],
                         turn)

            def output(l, s, c, turn=0):
                for n in range(NCH):
                    load(s + n, w_ffn_out[l][:, bass.ds(c * GK, GK), cols(n * COLS)], turn)

            def ffn(l):
                base = S_FFN[l]
                hidden(l, base, 0, 0)
                hidden(l, base + KG, 0, 1)
                sp.wait_ge(ln_chunk, NCH * (2 * l + 1))
                load_params(2 * l + 1)
                with sp.Fori(0, FC - 1) as turn:
                    s = base + 2 * KG
                    hidden(l, s, turn + 1, 0, turn)
                    output(l, s + KG, turn, turn)
                    hidden(l, s + 2 * KG, turn + 1, 1, turn)
                output(l, base + FFN_GROUPS - KG, FC - 1)

            for n in range(NCH):
                sp.dma_start(xres[:, :, cols(n * COLS)], x_t[:, :, cols(n * COLS)]).then_inc(x_landed[n], 16)
                if n < 2:
                    even_in(n)
            for n in range(2, RAW):
                even_in(n)
            sp.dma_start(prow2[0:8, 1], pool_scale[0].rearrange("(t p) -> t p", p=P)).then_inc(const_landed, 16)
            sp.dma_start(prow2[:, 0], attn_b_qkv[0, 0:18 * P].rearrange("(t p) -> t p", p=P)) \
                .then_inc(const_landed, 16)
            for l in range(2):
                for k in range(CONV):
                    sp.dma_start(prow[:, 4 * l + k], ffn_conv_w[l, k].rearrange("(t p) -> t p", p=P)) \
                        .then_inc(const_landed, 16)
                sp.dma_start(prow[:, 4 * l + 3], ffn_conv_b[l].rearrange("(t p) -> t p", p=P)) \
                    .then_inc(const_landed, 16)
            sp.dma_start(dec, decay).then_inc(const_landed, 16)
            sp.dma_start(tapsw, pool_taps).then_inc(const_landed, 16)
            sp.dma_start(pw[:], pool_w[0].rearrange("g (t p) n -> p g t n", p=P)).then_inc(const_landed, 16)
            sp.dma_start(sink_row[:], attn_sinks.to_broadcast([P, AH])).then_inc(const_landed, 16)
            for s in range(RAW, S_EVEN_OUT):
                even_in(s)
            for i in range(NCH * KG):
                n, kg = divmod(i, KG)
                kg = EVEN_OUT_KG[kg]
                load(S_EVEN_OUT + i, w_even_out[:, GK * kg:GK * kg + GK, cols(n * COLS)])
                if i == 4:
                    sp.wait_ge(t_ready, FILL_LN0)
                    load_params(0)
            ffn(0)
            for s in range(S_ODD_IN, S_ODD_OUT):
                c, kg = divmod(s - S_ODD_IN, KG)
                load(s, w_qkv[:, GK * kg:GK * kg + GK, cols(ODD_COLS[c])])
                if s == S_ODD_IN + 3:
                    sp.wait_ge(ln_chunk, NCH * 2)
                    sp.dma_start(dist, distance).then_inc(const_landed, 16)
                    sp.dma_start(v_bias, attn_b_qkv[0:1, 18 * P:20 * P].to_broadcast([P, 2 * P])) \
                        .then_inc(const_landed, 16)
            for i, (n, kg) in enumerate(ODD_OUT_ORDER):
                load(S_ODD_OUT + i, w_att_out[:, GK * kg:GK * kg + GK, cols(n * COLS)])
                if i == 12:
                    sp.wait_ge(t_ready, FILL_LN2)
                    load_params(2)
            ffn(1)
            for n in range(NCH):
                sp.wait_ge(ln_chunk, NCH * 3 + n + 1)
                sp.dma_start(out_t[:, :, cols(n * COLS)], xres[:, :, cols(n * COLS)]).then_inc(stored, 16)
            sp.wait_ge(stored, 16 * NCH)

        @block.gpsimd
        def _(pool):
            nc.gpsimd.memset(ident[:], 0.0).then_inc(ident_ready, 1)
            pool.wait_ge(ident_ready, 1)
            nc.gpsimd.affine_select(out=ident[:], in_=ident[:], compare_op=ALU.not_equal, fill=1.0, base=0,
                                    pattern=[[-1, P]], channel_multiplier=1).then_inc(ident_ready, 1)

            def scale(fills):
                pool.wait_ge(turned, fills)
                for a in range(TOK):
                    nc.gpsimd.tensor_scalar(xres[:, a], xres[:, a], ALPHA, 1.0, ALU.mult, ALU.mult) \
                        .then_inc(scaled, 1)

            scale(FILL_X + 8)
            scale(FILL_LN0 + 8)
            scale(FILL_LN1 + 8)
            scale(FILL_LN2 + 8)

        @block.scalar
        def _(act):
            def high(s, turn=0):
                if s >= S_END:
                    return
                act.wait_ge(raw_landed[s % RAW], 16 * (s // RAW + 1) + turn * (16 * (12 // RAW)))
                if not isinstance(turn, int) or s >= HI:
                    act.wait_ge(used, s - HI + 1 + turn * 12)
                nc.scalar.activation(w_hi[:, s % HI], raw[:, s % RAW], ACT.Copy).then_inc(hi_ready, 1)

            def fill_high(n, j):
                act.wait_ge(turned, n + 1)
                nc.scalar.activation(T[:, 2 * j:2 * j + 2, 0:SEQ],
                                     ps[:, fill_bank(n)].rearrange("p (t n) -> p t n", t=2),
                                     ACT.Copy).then_inc(t_hi, 1)

            def fill_all(first, s):
                for n in range(8):
                    fill_high(first + n, n)
                    if n == 1:
                        high(s + HI_LEAD)

            def halves(n, bank, ended, turn=0):
                act.wait_ge(used, ended + turn * 12)
                if not isinstance(turn, int) or n >= 2:
                    act.wait_ge(added, n - 1 + turn * 4)
                nc.scalar.activation(half[:, n % 2], ps[:, bank:bank + 2, SEQ:2 * SEQ], ACT.Copy) \
                    .then_inc(half_out, 1)

            def ln_root(m):
                act.wait_ge(var_ready, m + 2)
                nc.scalar.activation(rstd[:], rstd[:], ACT.Sqrt).then_inc(std_ready, 1)

            for s in range(HI_LEAD):
                high(s)
            fill_all(FILL_X, 0)
            for s in range(1, S_EVEN_OUT):
                c, kg = divmod(s, KG)
                if kg == 0 and 1 <= c <= 4:
                    for q in range(2):
                        halves(2 * (c - 1) + q, 4 * ((c - 1) % 2) + 2 * q, s)
                if kg == 0 and 5 <= c <= 8:
                    act.wait_ge(used, s)
                    to = (v_nat, u_nat)[(c - 5) // 2]
                    lo, b = COLS * ((c - 5) % 2), 2 * ((c - 5) % 2)
                    nc.scalar.activation(to[:, :, lo:lo + COLS], ps[:, b:b + 2], ACT.Copy).then_inc(vug_out, 1)
                if s == 4 * 9:
                    act.wait_ge(used, s)
                    act.wait_ge(ret_mixed, RH)
                    nc.scalar.activation(silu_g[:, :, 0:COLS], ps[:, 0:2], ACT.Silu).then_inc(vug_out, 1)
                high(s + HI_LEAD)
                if s == 3:
                    act.wait_ge(params_turned, 1)
                    for l in range(2):
                        nc.scalar.activation(taps[:, 4 * l:4 * l + 4],
                                             ps[:, 4 + l, 0:4 * FT].rearrange("p (t n) -> p t n", t=4), ACT.Copy) \
                            .then_inc(params_ready, 1)
                    nc.scalar.activation(qk_bias[:], ps[:, 6, 0:18], ACT.Copy).then_inc(params_ready, 1)
                    nc.scalar.activation(p_scale[:], ps[:, 6, 32:40], ACT.Copy).then_inc(params_ready, 1)
                hd = s - (RET_AT + 2)
                if 0 <= hd < RH:
                    act.wait_ge(ret_mixed, hd + 1)
                    nc.scalar.activation(y_nat[:, :, RD * hd:RD * hd + RD],
                                         ps[:, mix_bank(hd)].rearrange("p (a n) -> p a n", a=TOK), ACT.Copy) \
                        .then_inc(ret_out, 1)
                if s == RET_AT + 6:
                    act.wait_ge(var_ready, 1)
                    nc.scalar.activation(r_std[:], r_std[:], ACT.Sqrt).then_inc(std_ready, 1)
                i = s - (POOL_AT + 1)
                if 0 <= i < 2:
                    act.wait_ge(pooled, i + 1)
                    for n in (2 * i, 2 * i + 1):
                        nc.scalar.activation(pooledT[:, 2 * n:2 * n + 2],
                                             ps[:, 4 + n].rearrange("p (t n) -> p t n", t=2), ACT.Copy) \
                            .then_inc(pooled_out, 1)
                i = s - (POOL_AT + 3)
                if 0 <= i < 2:
                    act.wait_ge(pool_mixed, i + 1)
                    for n in range(4 * i, 4 * i + 4):
                        nc.scalar.activation(poolT[:, n], ps[:, 4 + n // 2, SEQ * (n % 2):SEQ * (n % 2) + SEQ],
                                             ACT.Copy, scale=p_scale[:, n:n + 1]).then_inc(pool_out, 1)

            act.wait_ge(used, S_EVEN_OUT)
            act.wait_ge(pool_out, 8)
            for i in range(2):
                nc.scalar.activation(T[:, 8 + 4 * i:12 + 4 * i, 0:SEQ], poolT[:, 4 * i:4 * i + 4], ACT.Copy) \
                    .then_inc(pool_hi, 1)
                if i == 0:
                    nc.scalar.activation(silu_g[:, :, COLS:2 * COLS], ps[:, 2:4], ACT.Silu).then_inc(vug_out, 1)
            for n in range(4):
                fill_high(FILL_RET + n, n)
            for s in range(S_EVEN_OUT, S_FFN0):
                high(s + HI_LEAD)

            def gelu(n, q, turn=0):
                act.wait_ge(conv_done, n + turn * 2)
                nc.scalar.activation(conv_g[:, 2 * q:2 * q + 2], conv_g[:, 2 * q:2 * q + 2], ACT.Gelu) \
                    .then_inc(gelu_out, 1)

            def gated_high(n, q, turn=0):
                act.wait_ge(gated_out, n + turn * 2)
                nc.scalar.activation(gT[:, 2 * q:2 * q + 2, 0:SEQ], gated[:, 2 * q:2 * q + 2], ACT.Copy) \
                    .then_inc(g_hi, 1)

            def feed_forward(l):
                base, tp, gp = S_FFN[l], TP_FFN[l], 2 * FC * l
                ln_root(2 * l)
                fill_all(FILL_LN[2 * l], base)
                for j in range(1, 8):
                    high(base + j + HI_LEAD)
                    if j == 4:
                        for q in range(2):
                            halves(tp + q, 2 * q, base + 4)
                    if j in (5, 6):
                        gelu(gp + j - 4, j - 5)
                with act.Fori(0, FC - 1) as turn:
                    s = base + 2 * KG
                    for j in range(12):
                        high(s + j + HI_LEAD, turn)
                        if j == 0:
                            for q in range(2):
                                halves(tp + 2 + q, 4 + 2 * q, s, turn)
                        if j == 4:
                            for q in range(2):
                                halves(tp + 4 + q, 2 * q, s + 4, turn)
                        if j in (1, 2):
                            gated_high(gp + j, j - 1, turn)
                        if j in (5, 6):
                            gelu(gp + 2 + j - 4, j - 5, turn)
                end = base + FFN_GROUPS - KG
                for q in range(2):
                    halves(tp + 4 * FC - 2 + q, 4 + 2 * q, end)
                    gated_high(gp + 2 * FC - 1 + q, q)
                for s in range(end, end + KG):
                    high(s + HI_LEAD)

            feed_forward(0)

            def attention(s):
                b = s - 1 - ATT_AT
                if 0 <= b - 1 < PAIRS:
                    act.wait_ge(att_turned, b)
                    nc.scalar.activation(PT, ps[:, 6:8, 0:3 * P], ACT.Copy).then_inc(att_pt, 1)
                if 0 <= b < PAIRS:
                    act.wait_ge(att_max, b + 1)
                    for a in range(2):
                        for blk, (lo, n) in enumerate(((0, P), (P, 2 * P))):
                            nc.scalar.activation(S[:, a, lo:lo + n], S[:, a, lo:lo + n], ACT.Exp,
                                                 bias=nm[:, b, a, blk:blk + 1],
                                                 accum_out=rs[:, b, a, blk:blk + 1])
                    nc.scalar.activation(es[:, b], es[:, b], ACT.Exp).then_inc(att_exp, 1)

            ln_root(1)
            fill_all(FILL_LN1, S_ODD_IN)
            for s in range(S_ODD_IN + 1, S_FFN1):
                if s == S_ODD_IN + KG:
                    halves(TP_ODD, 0, s)
                if s == S_ODD_IN + KG + 1:
                    act.wait_ge(akv_ready, 2)
                    act.dma_start(akT[64:128, 0:KVH:2], akT[0:64, 0:KVH:2]).then_inc(key_copied, 16)
                    act.dma_start(akT[0:64, 1:KVH:2], akT[64:128, 1:KVH:2]).then_inc(key_copied, 16)
                cc = (s - S_ODD_IN) // KG - 2
                if (s - S_ODD_IN) % KG == 0 and 0 <= cc < 4:
                    for q in range(2):
                        halves(TP_ODD + 1 + 2 * cc + q, 2 * q, s)
                if s in (S_ODD_OUT, S_ODD_OUT + 1):
                    for t in (0, 1):
                        j = 2 * (s - S_ODD_OUT) + t
                        fill_high(FILL_ATT + j, j)
                if s != S_ODD_OUT + 4:
                    high(s + HI_LEAD)
                    attention(s)
                if s == S_ODD_OUT + 4:
                    attention(s)
                    for j in (4, 5):
                        fill_high(FILL_ATT + j, j)
                    high(s + HI_LEAD)
                if s == S_ODD_OUT + 6:
                    for j in (6, 7):
                        fill_high(FILL_ATT + j, j)
            feed_forward(1)
            ln_root(3)

        @block.vector
        def _(dve):
            own = Count()
            vec = nc.vector

            def chain(ins):
                own.n += 1
                ins.then_inc(dve_step, 1)
                dve.wait_ge(dve_step, own.now())

            def low(s, turn=0):
                if s >= S_END:
                    return
                dve.wait_ge(hi_ready, s + 1 + turn * 12)
                if not isinstance(turn, int) or s >= LO:
                    dve.wait_ge(used, s - LO + 1 + turn * 12)
                vec.tensor_tensor(w_lo[:, s % LO], raw[:, s % RAW], w_hi[:, s % HI].bitcast(F32),
                                  ALU.subtract).then_inc(lo_ready, 1)

            def fill_low(n, j):
                dve.wait_ge(t_hi, n + 1)
                vec.tensor_tensor(T[:, 2 * j:2 * j + 2, SEQ:2 * SEQ],
                                  ps[:, fill_bank(n)].rearrange("p (t n) -> p t n", t=2),
                                  T[:, 2 * j:2 * j + 2, 0:SEQ].bitcast(F32), ALU.subtract).then_inc(t_ready, 1)

            def pair_sum(to, n, bank, turn=0):
                dve.wait_ge(half_out, n + 1 + turn * 4)
                vec.tensor_tensor(to, ps[:, bank:bank + 2, 0:SEQ], half[:, n % 2], ALU.add).then_inc(added, 1)

            def add_chunk(n, bank, count_in, last):
                ins = vec.tensor_tensor(xres[:, :, COLS * n:COLS * n + COLS],
                                        xres[:, :, COLS * n:COLS * n + COLS], ps[:, bank:bank + 2], ALU.add)
                ins.then_inc(count_in[0], 1)
                if last:
                    dve.wait_ge(*count_in)
                    for a in range(TOK):
                        vec.bn_stats(stats[:, a, n], xres[:, a, COLS * n:COLS * n + COLS])

            def layer_norm(m, fill, s):
                own.n += 1
                vec.memset(rstd[:], 0.0).then_inc(dve_step, 1)
                dve.wait_ge(dve_step, own.now())
                for a in range(TOK):
                    ins = vec.bn_aggr(mean_var[:, a], stats[:, a])
                chain(ins)
                vec.tensor_scalar(rstd[:], mean_var[:, :, 1], EPS, None, ALU.add).then_inc(var_ready, 1)
                dve.wait_ge(std_ready, m + 2)
                chain(vec.reciprocal(rstd[:], rstd[:]))
                dve.wait_ge(lnp_landed, 32 * (m + 1))
                for q in range(NCH):
                    c = slice(COLS * q, COLS * q + COLS)
                    for a in range(TOK):
                        ins = vec.scalar_tensor_tensor(xres[:, a, c], xres[:, a, c], mean_var[:, a, 0:1],
                                                       lnp[:, 0, c], ALU.subtract, ALU.mult)
                    chain(ins)
                    for a in range(TOK):
                        ins = vec.scalar_tensor_tensor(xres[:, a, c], xres[:, a, c], rstd[:, a:a + 1],
                                                       lnp[:, 1, c], ALU.mult, ALU.add)
                    ins.then_inc(ln_chunk, 1)
                    if fill is not None and q >= 1:
                        for n in (2 * q - 2, 2 * q - 1):
                            fill_low(fill + n, n)
                        if q == 1:
                            low(s + LO_LEAD)
                if fill is not None:
                    for n in (6, 7):
                        fill_low(fill + n, n)

            low(0)
            low(1)
            for n in range(8):
                fill_low(FILL_X + n, n)
                if n == 1:
                    low(LO_LEAD)
            for s in range(1, S_EVEN_OUT):
                c, kg = divmod(s, KG)
                if kg == 0 and 1 <= c <= 4:
                    for q in range(2):
                        to = (qT, kT)[(c - 1) // 2]
                        t = TPC * ((c - 1) % 2) + 2 * q
                        pair_sum(to[:, t:t + 2], 2 * (c - 1) + q, 4 * ((c - 1) % 2) + 2 * q)
                hd = s - (RET_AT + 1)
                if 0 <= hd < RH:
                    dve.wait_ge(ret_scored, hd + 1)
                    if hd == 0:
                        dve.wait_ge(const_landed, 16 * 14)
                    vec.tensor_tensor(probs[:, hd % 2], ps[:, ret_bank(hd), 0:3 * P], dec[:, hd], ALU.mult) \
                        .then_inc(ret_probs, 1)
                low(s + LO_LEAD)
                hd = s - (RET_AT + 2)
                if 0 <= hd < RH:
                    dve.wait_ge(ret_out, hd + 1)
                    for a in range(TOK):
                        ins = vec.bn_stats(r_stats[:, TOK * hd + a], y_nat[:, a, RD * hd:RD * hd + RD])
                    if hd == RH - 1:
                        chain(ins)
                        for i in range(TOK * RH):
                            ins = vec.bn_aggr(r_mv[:, i], r_stats[:, i])
                        chain(ins)
                        vec.tensor_scalar(r_std[:], r_mv[:, :, 1:2], EPS, None, ALU.add).then_inc(var_ready, 1)
                if s == RET_AT + 7:
                    dve.wait_ge(std_ready, 1)
                    chain(vec.reciprocal(r_std[:], r_std[:]))
                    for hd in range(RH):
                        for a in range(TOK):
                            i = TOK * hd + a
                            yy = y_nat[:, a, RD * hd:RD * hd + RD]
                            ins = vec.tensor_scalar(yy, yy, r_mv[:, i, 0:1], r_std[:, i], ALU.subtract, ALU.mult)
                    chain(ins)
                if s == 4 * 9:
                    dve.wait_ge(vug_out, 5)
                    vec.tensor_tensor(y_nat[:, :, 0:COLS], y_nat[:, :, 0:COLS], silu_g[:, :, 0:COLS], ALU.mult) \
                        .then_inc(ret_gated, 1)
                    for blk in range(2):
                        vec.tensor_scalar(neg_sink[:, :, blk], sink_row[:], -1.0, None, ALU.mult)
            for i in range(2):
                dve.wait_ge(pool_hi, i + 1)
                vec.tensor_tensor(T[:, 8 + 4 * i:12 + 4 * i, SEQ:2 * SEQ], poolT[:, 4 * i:4 * i + 4],
                                  T[:, 8 + 4 * i:12 + 4 * i, 0:SEQ].bitcast(F32), ALU.subtract) \
                    .then_inc(pool_ready, 1)
            dve.wait_ge(vug_out, 6)
            vec.tensor_tensor(y_nat[:, :, COLS:RW], y_nat[:, :, COLS:RW], silu_g[:, :, COLS:RW], ALU.mult) \
                .then_inc(ret_gated, 1)
            for n in range(4):
                fill_low(FILL_RET + n, n)
            for s in range(S_EVEN_OUT, S_FFN0):
                i = s - S_EVEN_OUT
                if i % KG == 0 and i:
                    n = i // KG - 1
                    dve.wait_ge(used, s)
                    dve.wait_ge(scaled, TOK)
                    add_chunk(n, 2 * (n % 2), (proj_added, n + 1), True)
                low(s + LO_LEAD)
            dve.wait_ge(used, S_FFN0)
            add_chunk(3, 2, (proj_added, 4), True)

            def convolve(kind, q, conv, cur, bank, n, turn=0, count_in=None):
                t = 2 * q
                pair_sum(h[:, t:t + 2, CONV - 1:], n, bank, turn)
                dve.wait_ge(added, n + 1 + turn * 4)
                for k in range(CONV):
                    for i in (t, t + 1):
                        if k == 0:
                            ins = vec.tensor_scalar(conv[:, i], h[:, i, 0:SEQ], cur[:, kind, 0, i:i + 1],
                                                    cur[:, kind, 3, i:i + 1], ALU.mult, ALU.add)
                        else:
                            ins = vec.scalar_tensor_tensor(conv[:, i], h[:, i, k:k + SEQ],
                                                           cur[:, kind, k, i:i + 1], conv[:, i],
                                                           ALU.mult, ALU.add)
                    if k < CONV - 1 or kind == 1:
                        chain(ins)
                    else:
                        ins.then_inc(conv_done, 1)

            def feed_forward(l):
                base, tp, gp = S_FFN[l], TP_FFN[l], 2 * FC * l
                outs = NCH * FC * l
                layer_norm(2 * l, FILL_LN[2 * l], base)
                chain(vec.memset(h[:, :, 0:CONV - 1], 0.0))

                def current(kind, first):
                    chain(vec.tensor_copy(cur[:, kind], taps[:, 4 * l:4 * l + 4, first]))

                def value_pair(q, n, g, turn=0):
                    convolve(1, q, conv_v, cur, 4 + 2 * q, n, turn)
                    dve.wait_ge(gelu_out, g + turn * 2)
                    vec.tensor_tensor(gated[:, 2 * q:2 * q + 2], conv_v[:, 2 * q:2 * q + 2],
                                      conv_g[:, 2 * q:2 * q + 2], ALU.mult).then_inc(gated_out, 1)

                def gated_low(q, g, turn=0):
                    dve.wait_ge(g_hi, g + turn * 2)
                    vec.tensor_tensor(gT[:, 2 * q:2 * q + 2, SEQ:2 * SEQ], gated[:, 2 * q:2 * q + 2],
                                      gT[:, 2 * q:2 * q + 2, 0:SEQ].bitcast(F32), ALU.subtract) \
                        .then_inc(g_ready, 1)

                for j in range(1, 8):
                    low(base + j + LO_LEAD)
                    if j == 4:
                        current(0, slice(0, TPC))
                    if j in (4, 5):
                        convolve(0, j - 4, conv_g, cur, 2 * (j - 4), tp + j - 4)
                with dve.Fori(0, FC - 1) as turn:
                    own.enter(turn, LOOP_OWN)
                    s = base + 2 * KG
                    for j in range(12):
                        if j == 8:
                            dve.wait_ge(used, s + 8 + turn * 12)
                            add_chunk(3, 6, (ffn_added,), False)
                        if j in (5, 6, 7):
                            dve.wait_ge(used, s + j + turn * 12)
                            if j == 5:
                                dve.wait_ge(scaled, TOK * (2 + 2 * l))
                            add_chunk(j - 5, 4 + 2 * ((j - 5) % 2), (ffn_added,), False)
                        low(s + j + LO_LEAD, turn)
                        if j == 0:
                            current(1, bass.ds(FT // 2 + turn * TPC, TPC))
                        if j in (0, 1):
                            value_pair(j, tp + 2 + j, gp + 1 + j, turn)
                        if j in (2, 3):
                            gated_low(j - 2, gp + j - 1, turn)
                        if j == 4:
                            current(0, bass.ds((turn + 1) * TPC, TPC))
                        if j in (4, 5):
                            convolve(0, j - 4, conv_g, cur, 2 * (j - 4), tp + j, turn)
                    own.leave(FC - 1)
                end = base + FFN_GROUPS - KG
                current(1, slice(FT - TPC, FT))
                for q in range(2):
                    value_pair(q, tp + 4 * FC - 2 + q, gp + 2 * FC - 1 + q)
                    gated_low(q, gp + 2 * FC - 1 + q)
                for j in range(KG):
                    if j:
                        dve.wait_ge(used, end + j)
                        add_chunk(j - 1, 4 + 2 * ((j - 1) % 2), (ffn_added, outs + NCH * (FC - 1) + j), True)
                    low(end + j + LO_LEAD)
                dve.wait_ge(used, end + KG)
                add_chunk(3, 6, (ffn_added, outs + NCH * FC), True)

            feed_forward(0)

            def attention_max(s):
                b = s - 1 - ATT_AT
                if not 0 <= b < PAIRS:
                    return
                dve.wait_ge(att_scored, b + 1)
                for a in range(2):
                    slope = 2.0 ** (-8.0 / AH * (2 * b + a + 1))
                    ins = vec.scalar_tensor_tensor(S[:, a], dist, slope, ps[:, 4 + a, 0:3 * P],
                                                   ALU.mult, ALU.add)
                ins.then_inc(att_biased, 1)
                dve.wait_ge(att_biased, b + 1)
                vec.tensor_reduce(m_pair[:, b, :, 0], S[:, :, 0:P], AX_X, ALU.max)
                chain(vec.tensor_reduce(m_pair[:, b, :, 1], S[:, :, P:3 * P], AX_X, ALU.max))
                chain(vec.scalar_tensor_tensor(nm[:, b], m_pair[:, b], -1.0, neg_sink[:, 2 * b:2 * b + 2],
                                               ALU.mult, ALU.min))
                vec.tensor_tensor(es[:, b], nm[:, b], neg_sink[:, 2 * b:2 * b + 2], ALU.subtract) \
                    .then_inc(att_max, 1)

            def attention_out(s):
                b = s - 1 - ATT_AT
                if 0 <= b - 1 < PAIRS:
                    dve.wait_ge(att_exp, b)
                    chain(vec.tensor_tensor(es[:, b - 1], rs[:, b - 1], es[:, b - 1], ALU.add))
                    chain(vec.reciprocal(rinv[:, b - 1], es[:, b - 1]))
                if 0 <= b - 2 < PAIRS:
                    p = b - 2
                    dve.wait_ge(att_mixed, p + 1)
                    if b - 1 < PAIRS:
                        dve.wait_ge(att_pt, b)
                    for a in range(2):
                        o = AD * (2 * p + a)
                        ins = vec.tensor_tensor(o_nat[:, :, o:o + AD],
                                                ps[:, 6 + a, 3 * P:4 * P].rearrange("p (b n) -> p b n", b=2),
                                                rinv[:, p, a].unsqueeze(2).to_broadcast([P, 2, AD]), ALU.mult)
                    ins.then_inc(att_out, 1)

            layer_norm(1, FILL_LN1, S_ODD_IN)
            for s in range(S_ODD_IN + 1, S_FFN1):
                cc = (s - S_ODD_IN) // KG - 2
                if s == S_ODD_IN + KG:
                    dve.wait_ge(half_out, TP_ODD + 1)
                    for t in range(2):
                        for hf in range(2):
                            r = slice(64 * hf, 64 * hf + 64)
                            ins = vec.scalar_tensor_tensor(akT[r, 2 * t + hf], ps[r, t, 0:SEQ],
                                                           qk_bias[r, 16 + t:17 + t], half[r, TP_ODD % 2, t],
                                                           ALU.add, ALU.add)
                    ins.then_inc(added, 1)
                    dve.wait_ge(added, TP_ODD + 1)
                    for hf in range(2):
                        r = slice(64 * hf, 64 * hf + 64)
                        vec.tensor_scalar(akT[r, hf:KVH:2], akT[r, hf:KVH:2], AD ** -0.5, None, ALU.mult) \
                            .then_inc(akv_ready, 1)
                    dve.wait_ge(const_landed, 16 * 16)
                    for a in range(TOK):
                        ins = vec.tensor_tensor(av[:, a], ps[:, 2 + a, 0:SEQ], v_bias, ALU.add)
                    ins.then_inc(akv_ready, 1)
                if (s - S_ODD_IN) % KG == 0 and 0 <= cc < 4:
                    for q in range(2):
                        n = TP_ODD + 1 + 2 * cc + q
                        dve.wait_ge(half_out, n + 1)
                        for i in range(2):
                            t = TPC * cc + 2 * q + i
                            ins = vec.scalar_tensor_tensor(aqT[:, t], ps[:, 2 * q + i, 0:SEQ],
                                                           qk_bias[:, t:t + 1], half[:, n % 2, i],
                                                           ALU.add, ALU.add)
                        ins.then_inc(added, 1)
                if s in (S_ODD_OUT, S_ODD_OUT + 1):
                    for t in (0, 1):
                        j = 2 * (s - S_ODD_OUT) + t
                        fill_low(FILL_ATT + j, j)
                i = s - S_ODD_OUT
                if i in (7, 8, 12):
                    n = {7: 0, 8: 1, 12: 2}[i]
                    dve.wait_ge(used, s)
                    dve.wait_ge(scaled, TOK * 3)
                    add_chunk(n, 2 * (n % 2), (proj_added, NCH + n + 1), True)
                attention_max(s)
                if i == 4:
                    for j in (4, 5):
                        fill_low(FILL_ATT + j, j)
                low(s + LO_LEAD)
                attention_out(s)
                if i == 6:
                    for j in (6, 7):
                        fill_low(FILL_ATT + j, j)
            dve.wait_ge(used, S_FFN1)
            add_chunk(3, 2, (proj_added, 2 * NCH), True)
            feed_forward(1)
            layer_norm(3, None, None)

        @block.tensor
        def _(pe):
            mm = nc.tensor.matmul

            def ready(s, turn=0):
                pe.wait_ge(lo_ready, s + 1 + turn * 12)

            def turned_tile(s, kg, bank, j):
                for k in range(GK):
                    t = GK * kg + k
                    c = slice(P * j, P * j + P)
                    mm(ps[:, bank], w_hi[:, s % HI, k, c], T[:, t], start=kg == 0 and k == 0, stop=False)
                    ins = mm(ps[:, bank, 0:SEQ], w_lo[:, s % LO, k, c], T[:, t, 0:SEQ], start=False,
                             stop=kg == KG - 1 and k == GK - 1)
                return ins

            def plain_tile(s, src, first_tile, bank, a, start, stop, c=slice(0, COLS)):
                n = c.stop - c.start
                for k in range(GK):
                    t = first_tile + k
                    x_hi = src[:, t, P * a:P * a + P]
                    x_lo = src[:, t, SEQ + P * a:SEQ + P * a + P]
                    mm(ps[:, bank, 0:n], x_hi, w_hi[:, s % HI, k, c], start=start and k == 0, stop=False)
                    mm(ps[:, bank, 0:n], x_hi, w_lo[:, s % LO, k, c], start=False, stop=False)
                    ins = mm(ps[:, bank, 0:n], x_lo, w_hi[:, s % HI, k, c], start=False,
                             stop=stop and k == GK - 1)
                return ins

            def turn_pair(n, j, source):
                b = fill_bank(n)
                for t in range(2):
                    for a in range(TOK):
                        c = P * (2 * j + t)
                        ins = nc.tensor.transpose(ps[:, b, SEQ * t + P * a:SEQ * t + P * a + P],
                                                  source[:, a, c:c + P], ident[:])
                ins.then_inc(turned, 1)

            def turn_quarter(first, q, m):
                if m is None:
                    pe.wait_ge(x_landed[q], 16)
                else:
                    pe.wait_ge(ln_chunk, NCH * m + q + 1)
                if q >= 2 or m is not None:
                    pe.wait_ge(t_ready, first + 2 * q - 2)
                for j in (2 * q, 2 * q + 1):
                    turn_pair(first + j, j, xres)

            def first_chunk(s0, first, m, group):
                turn_quarter(first, 0, m)
                for kg in range(KG):
                    pe.wait_ge(t_ready, first + 2 * kg + 2)
                    ready(s0 + kg)
                    group(kg, 0)
                    if kg < KG - 1:
                        turn_quarter(first, kg + 1, m)
                    group(kg, 1).then_inc(used, 1)

            def turned_half(s0):
                def group(kg, part):
                    turned_tile(s0 + kg, kg, 2 * part, 2 * part)
                    return turned_tile(s0 + kg, kg, 2 * part + 1, 2 * part + 1)
                return group

            pe.wait_ge(ident_ready, 2)
            first_chunk(0, FILL_X, None, turned_half(0))
            pe.wait_ge(const_landed, 16 * 14)
            pe.wait_ge(t_ready, FILL_X + 8)
            for i in range(8):
                nc.tensor.transpose(ps[:, 4 + i // 4, FT * (i % 4):FT * (i % 4) + FT], prow[:, i],
                                    ident[0:FT, 0:FT])
            nc.tensor.transpose(ps[:, 6, 0:18], prow2[:, 0], ident[0:18, 0:18])
            nc.tensor.transpose(ps[:, 6, 32:40], prow2[0:8, 1], ident[0:8, 0:8]).then_inc(params_turned, 1)
            for s in range(KG, S_EVEN_OUT):
                c, kg = divmod(s, KG)
                if kg == 0:
                    if c == 1:
                        pe.wait_ge(params_ready, 4)
                    elif c <= 5:
                        pe.wait_ge(added, 2 * min(c - 1, 3))
                    elif c <= 9:
                        pe.wait_ge(vug_out, c - 5)
                ready(s)
                if c < 4:
                    for j in range(TPC):
                        ins = turned_tile(s, kg, 4 * (c % 2) + j, j)
                else:
                    for a in range(TOK):
                        ins = plain_tile(s, T, GK * kg, 2 * (c % 2) + a, a, kg == 0, kg == KG - 1)
                ins.then_inc(used, 1)

                hd = s - (RET_AT + 1)
                if 0 <= hd < RH:
                    pe.wait_ge(ret_probs, hd + 1)
                    pe.wait_ge(vug_out, 2)
                    if hd >= 2:
                        pe.wait_ge(ret_out, hd - 1)
                    b, v = mix_bank(hd), slice(RD * hd, RD * hd + RD)
                    mm(ps[:, b, 0:RD], probs[:, hd % 2, 0:P], v_nat[:, 0, v], start=True, stop=True)
                    mm(ps[:, b, RD:2 * RD], probs[:, hd % 2, P:2 * P], v_nat[:, 0, v], start=True, stop=False)
                    mm(ps[:, b, RD:2 * RD], probs[:, hd % 2, 2 * P:3 * P], v_nat[:, 1, v], start=False,
                       stop=True).then_inc(ret_mixed, 1)
                hd = s - RET_AT
                if 0 <= hd < RH:
                    pe.wait_ge(added, 8)
                    if hd >= 2:
                        pe.wait_ge(ret_probs, hd - 1)
                    b = ret_bank(hd)
                    for d in range(2):
                        mm(ps[:, b, 0:SEQ], kT[:, 2 * hd + d, 0:P], qT[:, 2 * hd + d], start=d == 0, stop=d == 1)
                    for d in range(2):
                        ins = mm(ps[:, b, SEQ:SEQ + P], kT[:, 2 * hd + d, P:SEQ], qT[:, 2 * hd + d, P:SEQ],
                                 start=d == 0, stop=d == 1)
                    ins.then_inc(ret_scored, 1)
                i = s - POOL_AT
                if 0 <= i < 2:
                    pe.wait_ge(vug_out, 4)
                    pe.wait_ge(ret_out, RH)
                    for n in range(4 * i, 4 * i + 4):
                        b, lo = 4 + n // 2, SEQ * (n % 2)
                        mm(ps[:, b, lo:lo + SEQ], u_nat[:, 0, P * n:P * n + P], tapsw[:, n // 2, 0:SEQ],
                           start=True, stop=False)
                        ins = mm(ps[:, b, lo + P:lo + SEQ], u_nat[:, 1, P * n:P * n + P],
                                 tapsw[:, n // 2, SEQ:SEQ + P], start=False, stop=True)
                    ins.then_inc(pooled, 1)
                i = s - (POOL_AT + 2)
                if 0 <= i < 2:
                    pe.wait_ge(pooled_out, 2 * i + 2)
                    for n in range(4 * i, 4 * i + 4):
                        b, lo = 4 + n // 2, SEQ * (n % 2)
                        for k in range(2):
                            ins = mm(ps[:, b, lo:lo + SEQ], pw[:, n // 2, k, P * (n % 2):P * (n % 2) + P],
                                     pooledT[:, 2 * (n // 2) + k], start=k == 0, stop=k == 1)
                    ins.then_inc(pool_mixed, 1)
                if s == S_EVEN_OUT - 2:
                    pe.wait_ge(pool_out, 8)
                    pe.wait_ge(ret_gated, 1)
                    for j in range(2):
                        turn_pair(FILL_RET + j, j, y_nat)

            def projection(s, n, kg, first, last):
                for a in range(TOK):
                    ins = plain_tile(s, T, GK * kg, 2 * (n % 2) + a, a, first, last)
                ins.then_inc(used, 1)

            for i in range(NCH * KG):
                s, n, pos = S_EVEN_OUT + i, i // KG, i % KG
                kg = EVEN_OUT_KG[pos]
                if pos == 0:
                    if n < 2:
                        pe.wait_ge(vug_out, 5 + n)
                    else:
                        pe.wait_ge(proj_added, n - 1)
                if n == 0:
                    if pos < 2:
                        pe.wait_ge(pool_ready, pos + 1)
                    else:
                        pe.wait_ge(t_ready, FILL_RET + 2 * (pos - 1))
                ready(s)
                projection(s, n, kg, pos == 0, pos == KG - 1)
                if i == 0:
                    pe.wait_ge(ret_gated, 2)
                    for j in (2, 3):
                        turn_pair(FILL_RET + j, j, y_nat)

            def feed_forward(l):
                base, tp, gp, outs = S_FFN[l], TP_FFN[l], 2 * FC * l, NCH * FC * l
                first = FILL_LN[2 * l]
                first_chunk(base, first, 2 * l, turned_half(base))
                pe.wait_ge(t_ready, first + 8)

                def hidden(s, bank, turn=0, waits=()):
                    for kg in range(KG):
                        ready(s + kg, turn)
                        for j in range(TPC):
                            if kg == 0 and waits and j % 2 == 0:
                                pe.wait_ge(*waits[j // 2])
                            ins = turned_tile(s + kg, kg, bank + j, j)
                        ins.then_inc(used, 1)

                def output(s, c4, c2, turn=0):
                    pe.wait_ge(g_ready, gp + 2 + c2)
                    for n in range(NCH):
                        if n < 2:
                            pe.wait_ge(added, tp + 3 + n + c4)
                        else:
                            pe.wait_ge(ffn_added, outs + n - 1 + c4)
                        ready(s + n, turn)
                        b = 4 + 2 * (n % 2)
                        for a in range(TOK):
                            ins = plain_tile(s + n, gT, 0, b + a, a, True, True)
                        ins.then_inc(used, 1)

                hidden(base + KG, 4)
                with pe.Fori(0, FC - 1) as turn:
                    s = base + 2 * KG
                    pe.wait_ge(added, tp + 2 + turn * 4)
                    hidden(s, 0, turn)
                    output(s + KG, turn * 4, turn * 2, turn)
                    hidden(s + 2 * KG, 4, turn, ((ffn_added, outs + 3 + turn * 4), (ffn_added, outs + 4 + turn * 4)))
                output(base + FFN_GROUPS - KG, 4 * (FC - 1), 2 * (FC - 1))

            feed_forward(0)

            def kv_half(kg, part):
                s = S_ODD_IN + kg
                if part == 0:
                    for j in range(2):
                        ins = turned_tile(s, kg, j, j)
                else:
                    for a in range(TOK):
                        ins = plain_tile(s, T, GK * kg, 2 + a, a, kg == 0, kg == KG - 1, slice(2 * P, 4 * P))
                return ins

            def burst(b):
                if 0 <= b - 2 < PAIRS:
                    p = b - 2
                    pe.wait_ge(att_pt, p + 1)
                    if p >= 1:
                        pe.wait_ge(att_out, p)
                    for a in range(2):
                        lo, kv = 3 * P, slice(AD * (p // 4), AD * (p // 4) + AD)
                        mm(ps[:, 6 + a, lo:lo + AD], PT[:, a, 0:P], av[:, 0, kv], start=True, stop=True)
                        mm(ps[:, 6 + a, lo + AD:lo + 2 * AD], PT[:, a, P:2 * P], av[:, 0, kv],
                           start=True, stop=False)
                        ins = mm(ps[:, 6 + a, lo + AD:lo + 2 * AD], PT[:, a, 2 * P:3 * P], av[:, 1, kv],
                                 start=False, stop=True)
                    ins.then_inc(att_mixed, 1)
                if 0 <= b - 1 < PAIRS:
                    pe.wait_ge(att_exp, b)
                    for a in range(2):
                        for i in range(3):
                            ins = nc.tensor.transpose(ps[:, 6 + a, P * i:P * i + P], S[:, a, P * i:P * i + P],
                                                      ident[:])
                    ins.then_inc(att_turned, 1)
                if b < PAIRS:
                    pe.wait_ge(added, TP_ODD + 1 + 2 * (b // 4 + 1))
                    if b == 0:
                        pe.wait_ge(akv_ready, 3)
                        pe.wait_ge(key_copied, 32)
                    else:
                        pe.wait_ge(att_biased, b)
                    for a in range(2):
                        r, kv = slice(64 * a, 64 * a + 64), b // 4
                        mm(ps[:, 4 + a, 0:P], aqT[r, b, 0:P], akT[r, kv, 0:P], start=True, stop=True)
                        ins = mm(ps[:, 4 + a, P:3 * P], aqT[r, b, P:SEQ], akT[r, kv], start=True, stop=True)
                    ins.then_inc(att_scored, 1)

            first_chunk(S_ODD_IN, FILL_LN1, 1, kv_half)
            pe.wait_ge(t_ready, FILL_LN1 + 8)
            for s in range(S_ODD_IN + KG, S_ODD_OUT):
                c, kg = divmod(s - S_ODD_IN - KG, KG)
                ready(s)
                for j in range(TPC):
                    if kg == 0 and j % 2 == 0:
                        if c == 0:
                            pe.wait_ge(added, TP_ODD + 1) if j == 0 else pe.wait_ge(akv_ready, 3)
                        else:
                            pe.wait_ge(added, TP_ODD + 1 + 2 * (c - 1) + 1 + j // 2)
                    ins = turned_tile(s, kg, j, j)
                ins.then_inc(used, 1)
                if s >= ATT_AT:
                    burst(s - ATT_AT)

            def turn_output(j):
                pe.wait_ge(att_out, 2 * j + 2)
                turn_pair(FILL_ATT + j, j, o_nat)

            for i, (n, kg) in enumerate(ODD_OUT_ORDER):
                s = S_ODD_OUT + i
                if i == 0:
                    pe.wait_ge(added, TP_ODD + 9)
                if i == 4:
                    pe.wait_ge(att_biased, PAIRS)
                if i in (0, 1, 4, 6):
                    j = {0: 0, 1: 2, 4: 4, 6: 6}[i]
                    if j in (2, 6):
                        pe.wait_ge(t_ready, FILL_ATT + j)
                    turn_output(j)
                    turn_output(j + 1)
                    pe.wait_ge(t_ready, FILL_ATT + j + 2)
                if kg == 0 and n >= 2:
                    pe.wait_ge(proj_added, NCH + n - 1)
                ready(s)
                projection(s, n, kg, kg == 0, kg == KG - 1)
                if s - ATT_AT < BURSTS:
                    burst(s - ATT_AT)
            feed_forward(1)


_INS = ["x", "ln_gain", "ln_bias", "even_w_in", "pool_w", "pool_scale", "even_w_out", "attn_w_qkv", "attn_b_qkv",
        "attn_sinks", "attn_w_out", "ffn_w_in", "ffn_conv_w", "ffn_conv_b", "ffn_w_out"]


def shape_tables():
    s, t = np.arange(P)[:, None], np.arange(SEQ)[None, :]
    log_gamma = np.log1p(-(2.0 ** (-5.0 - np.arange(RH))))
    lag = (t - s)[None]
    full = np.where(lag >= 0, np.exp(log_gamma[:, None, None] * np.maximum(lag, 0)), 0.0) * RD ** -0.5
    decay = np.concatenate([full, full[:, :, :P]], axis=2).transpose(1, 0, 2)
    w = np.array(WINDOWS)[:, None, None]
    inside = (lag >= 0) & (lag < w)
    mean = inside / np.minimum(t + 1, w) - (lag == 0)
    later = (inside / w - (lag == 0))[:, :, :P]
    taps = np.concatenate([mean, later], axis=2).transpose(1, 0, 2)
    i, j = np.arange(P)[:, None], np.arange(P)[None, :]
    own_block = np.where(j <= i, j - i, MASKED)
    before = np.where(j > i, j - i - P, MASKED)
    dist = np.concatenate([own_block, before, own_block], axis=1)
    return {n: np.ascontiguousarray(a, dtype=np.float32)
            for n, a in (("decay", decay), ("pool_taps", taps), ("distance", dist))}


def kernel(**inputs):
    import concourse.bacc as bacc
    from concourse.bass_utils import run_bass_kernel_spmd

    nc = bacc.Bacc("TRN2", target_bir_lowering=False, num_devices=1, dynamic_dma_scratch_size=1024)
    arrays, args = {}, []
    for name in _INS:
        a = np.ascontiguousarray(inputs[name])
        arrays[name] = a
        args.append(nc.dram_tensor(name, a.shape, mybir.dt.from_np(a.dtype), kind="ExternalInput").ap())
    for name, a in shape_tables().items():
        arrays[name] = a
        args.append(nc.dram_tensor(name, a.shape, F32, kind="ExternalInput").ap())
    args.append(nc.dram_tensor("out", (1, SEQ, D), F32, kind="ExternalOutput").ap())
    build_trunk(nc, *args)
    r = run_bass_kernel_spmd(nc, [arrays], core_ids=[0])
    return r.results[0]["out"]
```

```python
from contextlib import ExitStack

import numpy as np

import concourse.bass as bass
from concourse import mybir

F32 = mybir.dt.float32
F32R = mybir.dt.float32r
ALU = mybir.AluOpType
ACT = mybir.ActivationFunctionType
AX_X = mybir.AxisListType.X

P = 128
SEQ, D = 256, 2048
TOK = SEQ // P
KT = D // P
COLS = 512
GK = 4
KG = KT // GK
NCH = D // COLS
D_FF = 5632
FC = D_FF // COLS
FT = 2 * D_FF // P
TPC = COLS // P
CONV = 3
ALPHA = 4 ** 0.25
EPS = 1e-5
RH, RD = 4, 256
RW = RH * RD
WINDOWS = (2, 4, 8, 16)
AH, AD, KVH = 32, 64, 4
PAIRS = AH // 2
MASKED = -1e37
CONSTS = 16 * 16
ARENA = 14080

RAW, HI, LO = 4, 4, 3
HI_LEAD, LO_LEAD = 3, 2

EVEN_COLS = [0, 512, 1024, 1536, 2048, 2560, 4096, 4608, 3072, 3584]
EVEN_OUT_KG = [2, 3, 0, 1]
ODD_COLS = [2048, 0, 512, 1024, 1536]
ODD_OUT_ORDER = [(0, 0), (0, 1), (1, 0), (1, 1), (0, 2), (1, 2), (2, 0), (0, 3), (1, 3), (2, 1), (2, 2), (2, 3)] + \
                [(3, kg) for kg in range(KG)]
ODD_OUT_BANKS = [0, 2, 6, 0]
ODD_OUT_ENDS = {8: 0, 9: 1, 12: 2}
S_EVEN_IN = 0
S_EVEN_OUT = S_EVEN_IN + len(EVEN_COLS) * KG
S_FFN0 = S_EVEN_OUT + NCH * KG
FFN_GROUPS = 3 * KG * FC
S_ODD_IN = S_FFN0 + FFN_GROUPS
S_ODD_OUT = S_ODD_IN + len(ODD_COLS) * KG
S_FFN1 = S_ODD_OUT + NCH * KG
S_END = S_FFN1 + FFN_GROUPS
S_FFN = [S_FFN0, S_FFN1]

FILL_X, FILL_RET, FILL_LN0, FILL_LN1, FILL_ATT, FILL_LN2 = 0, 8, 12, 20, 28, 36
FILL_LN = [FILL_LN0, FILL_LN1, FILL_LN2]
ATT_FILL_BANKS = [2, 3, 2, 3, 4, 5, 4, 5]
ATT_FILL_AT = {0: 0, 1: 2, 4: 4, 6: 6}
SPLIT_AFTER = {1: 0, 5: 1, 7: 2}


def fill_bank(n):
    if FILL_ATT <= n < FILL_LN2:
        return ATT_FILL_BANKS[n - FILL_ATT]
    return 4 + n % 4


TP_EVEN = 0
TP_FFN0 = TP_EVEN + 8
TP_ODD = TP_FFN0 + 4 * FC
TP_FFN1 = TP_ODD + 1 + KT // 2
TP_FFN = [TP_FFN0, TP_FFN1]

RET_AT = 24
PARAMS_AT = 19
POOL_AT = 32
ATT_AT = S_ODD_IN + 2 * KG
BURSTS = PAIRS + 2
TURNS = FC - 2
LOOP_OWN = 12


class Count:

    def __init__(self):
        self.n, self.turn, self.per, self.start = 0, None, 0, 0

    def now(self):
        return self.n if self.turn is None else self.n + self.turn * self.per

    def enter(self, turn, per):
        self.turn, self.per, self.start = turn, per, self.n

    def leave(self, turns):
        assert self.n - self.start == self.per, (self.n - self.start, self.per)
        self.n, self.turn = self.start + self.per * turns, None


def build_trunk(nc, x, ln_gain, ln_bias, even_w_in, pool_w, pool_scale, even_w_out, attn_w_qkv, attn_b_qkv,
                attn_sinks, attn_w_out, ffn_w_in, ffn_conv_w, ffn_conv_b, ffn_w_out,
                decay, pool_taps, distance, out):
    tiled = lambda w: w.rearrange("(t p) n -> p t n", p=P)
    w_even_in, w_even_out = tiled(even_w_in[0]), tiled(even_w_out[0])
    w_qkv, w_att_out = tiled(attn_w_qkv[0]), tiled(attn_w_out[0])
    w_ffn_in = [tiled(ffn_w_in[l]) for l in range(2)]
    w_ffn_out = [tiled(ffn_w_out[l]) for l in range(2)]
    x_t = x[0].rearrange("(a p) d -> p a d", p=P)
    out_t = out[0].rearrange("(a p) d -> p a d", p=P)

    with ExitStack() as ctx:
        sb = lambda name, shape, dt=F32: ctx.enter_context(nc.sbuf_tensor(name, shape, dt))
        sem = lambda name: ctx.enter_context(nc.semaphore(name))

        xres = sb("xres", [P, TOK, D])
        T = sb("T", [P, KT, 2 * SEQ], F32R)
        raw = sb("raw", [P, RAW, GK, COLS])
        w_hi = sb("w_hi", [P, HI, GK, COLS], F32R)
        w_lo = sb("w_lo", [P, LO, GK, COLS], F32R)
        gT = sb("gT", [P, TPC, 2 * SEQ], F32R)
        ident = sb("ident", [P, P])
        taps = sb("taps", [P, 8, FT])
        qk_bias = sb("qk_bias", [P, 18])
        p_scale = sb("p_scale", [P, 8])
        ln_cols = sb("ln_cols", [P, 2, 4 * KT])
        stats = sb("stats", [P, TOK, NCH, 6])
        mean_var = sb("mean_var", [P, TOK, 2])
        rstd = sb("rstd", [P, TOK])
        shift = sb("shift", [P, 1])
        arena = sb("arena", [P, ARENA])

        used_words = [0]

        def take(*shape):
            n = int(np.prod(shape))
            a = arena[:, used_words[0]:used_words[0] + n]
            used_words[0] += n
            assert used_words[0] <= ARENA, used_words[0]
            names = "abcd"[:len(shape)]
            if len(shape) > 1:
                a = a.rearrange(f"p ({' '.join(names)}) -> p {' '.join(names)}",
                                **{c: s for c, s in zip(names, shape)})
            return a

        qT = take(8, SEQ)
        kT = take(8, SEQ)
        v_nat = take(TOK, RW)
        u_nat = take(TOK, RW)
        y_nat = take(TOK, RW)
        rows = y_nat[:, 0].rearrange("p (t n) -> p t n", n=P)
        rows2 = y_nat[:, 1].rearrange("p (t n) -> p t n", n=P)
        prow, prow2, ln_rows = rows[0:FT], rows2[0:18], rows2[0:4 * KT, 2:4]
        probs = take(2, 3 * P)
        dec = take(RH, 3 * P)
        tapsw = take(4, 3 * P)
        pw = sb("pw", [P, 4, 2, 256])
        pooledT = qT
        poolT = kT
        silu_g = v_nat
        r_stats = sb("r_stats", [P, TOK * RH, 6])
        r_mv = sb("r_mv", [P, TOK * RH, 2])
        r_std = sb("r_std", [P, TOK * RH, 1])
        used_words[0] = 0
        aqT = take(KT, SEQ)
        akT = take(KVH, SEQ)
        o_nat = take(TOK, D)
        av = take(TOK, KVH * AD)
        S = take(2, 3 * P)
        PT = take(2, 3 * P)
        dist = take(3 * P)
        v_bias = take(KVH * AD)
        m_pair, nm, es, rs, rinv = (sb(f"att{i}", [P, PAIRS, 2, 2]) for i in range(5))
        neg_sink = sb("neg_sink", [P, AH, 2])
        sink_row = sb("sink_row", [P, AH])
        used_words[0] = 0
        lnp = take(2, D)
        half = sb("half", [P, 2, 2, SEQ])
        h = take(TPC, CONV - 1 + SEQ)
        conv_g = take(TPC, SEQ)
        conv_v = take(TPC, SEQ)
        gated = take(TPC, SEQ)
        cur = sb("cur", [P, 2, 4, TPC])

        ps = ctx.enter_context(nc.psum_tensor("ps", [P, 8, COLS], F32))

        raw_landed = [sem(f"raw_landed{i}") for i in range(RAW)]
        x_landed = [sem(f"x_landed{i}") for i in range(NCH)]
        const_landed = sem("const_landed")
        lnp_landed = sem("lnp_landed")
        stored = sem("stored")
        key_copied = sem("key_copied")
        ident_ready = sem("ident_ready")
        scaled = sem("scaled")
        hi_ready = sem("hi_ready")
        lo_ready = sem("lo_ready")
        first_landed = [sem(f"first_landed{k}") for k in range(GK - 1)]
        first_hi = sem("first_hi")
        first_lo = sem("first_lo")
        used = sem("used")
        turned = sem("turned")
        t_hi = sem("t_hi")
        t_ready = sem("t_ready")
        params_turned = sem("params_turned")
        params_ready = sem("params_ready")
        half_out = sem("half_out")
        added = sem("added")
        vug_out = sem("vug_out")
        ret_scored = sem("ret_scored")
        ret_probs = sem("ret_probs")
        ret_mixed = sem("ret_mixed")
        ret_out = sem("ret_out")
        ret_gated = sem("ret_gated")
        pooled = sem("pooled")
        pooled_out = sem("pooled_out")
        pool_mixed = sem("pool_mixed")
        pool_out = sem("pool_out")
        pool_hi = sem("pool_hi")
        pool_ready = sem("pool_ready")
        proj_added = sem("proj_added")
        var_ready = sem("var_ready")
        std_ready = sem("std_ready")
        ln_chunk = sem("ln_chunk")
        conv_done = sem("conv_done")
        gelu_out = sem("gelu_out")
        gated_out = sem("gated_out")
        g_hi = sem("g_hi")
        g_ready = sem("g_ready")
        ffn_added = sem("ffn_added")
        akv_ready = sem("akv_ready")
        att_scored = sem("att_scored")
        att_biased = sem("att_biased")
        att_max = sem("att_max")
        att_exp = sem("att_exp")
        att_turned = sem("att_turned")
        att_pt = sem("att_pt")
        att_mixed = sem("att_mixed")
        att_out = sem("att_out")
        last_half = sem("last_half")
        shift_ready = sem("shift_ready")
        last_normed = sem("last_normed")
        last_scaled = sem("last_scaled")
        last_first = sem("last_first")
        last_second = sem("last_second")
        act_step = sem("act_step")
        pool_step = sem("pool_step")
        dve_step = sem("dve_step")

        block = ctx.enter_context(nc.Block())

        ret_bank = lambda hd: 4 + hd % 2
        mix_bank = lambda hd: 6 + hd % 2
        q_bank = lambda c: 4 if c == 0 else 0

        @block.sync
        def _(sp):
            def load(s, source, turn=0):
                if not isinstance(turn, int) or s >= RAW:
                    sp.wait_ge(lo_ready, s - RAW + 1 + turn * 12)
                sp.dma_start(raw[:, s % RAW], source).then_inc(raw_landed[s % RAW], 16)

            def load_params(m):
                l, which = divmod(m, 2)
                sp.dma_start(lnp[:, 0], ln_gain[l, which:which + 1, :].to_broadcast([P, D])) \
                    .then_inc(lnp_landed, 16)
                sp.dma_start(lnp[:, 1], ln_bias[l, which:which + 1, :].to_broadcast([P, D])) \
                    .then_inc(lnp_landed, 16)

            def cols(c, n=COLS):
                return slice(c, c + n)

            def even_in(s):
                c, kg = divmod(s - S_EVEN_IN, KG)
                load(s, w_even_in[:, GK * kg:GK * kg + GK, cols(EVEN_COLS[c])])

            def hidden(l, s, c, value, turn=0):
                for kg in range(KG):
                    load(s + kg, w_ffn_in[l][:, GK * kg:GK * kg + GK, bass.ds(c * COLS + value * D_FF, COLS)],
                         turn)

            def output(l, s, c, turn=0):
                for n in range(NCH):
                    load(s + n, w_ffn_out[l][:, bass.ds(c * GK, GK), cols(n * COLS)], turn)

            def ffn(l):
                base = S_FFN[l]
                hidden(l, base, 0, 0)
                hidden(l, base + KG, 0, 1)
                hidden(l, base + 2 * KG, 1, 0)
                output(l, base + 3 * KG, 0)
                sp.wait_ge(scaled, TOK * (2 * l + 2))
                load_params(2 * l + 1)
                hidden(l, base + 4 * KG, 1, 1)
                with sp.Fori(1, TURNS) as turn:
                    s = base + 2 * KG
                    hidden(l, s, turn + 1, 0, turn)
                    output(l, s + KG, turn, turn)
                    hidden(l, s + 2 * KG, turn + 1, 1, turn)
                tail = base + FFN_GROUPS - 4 * KG
                hidden(l, tail, FC - 1, 0)
                hidden(l, tail + KG, FC - 1, 1)
                output(l, tail + 2 * KG, FC - 2)
                output(l, tail + 3 * KG, FC - 1)

            for n in range(NCH):
                sp.dma_start(xres[:, :, cols(n * COLS)], x_t[:, :, cols(n * COLS)]).then_inc(x_landed[n], 16)
                if n == 0:
                    for k in range(GK):
                        sp.dma_start(raw[:, 0, k], w_even_in[:, k, cols(EVEN_COLS[0])]) \
                            .then_inc(first_landed[k] if k < GK - 1 else raw_landed[0], 16)
                else:
                    even_in(n)
            for s in range(RAW, 10):
                even_in(s)
            sp.dma_start(prow2[0:8, 1], pool_scale[0].rearrange("(t p) -> t p", p=P)).then_inc(const_landed, 16)
            sp.dma_start(prow2[:, 0], attn_b_qkv[0, 0:18 * P].rearrange("(t p) -> t p", p=P)) \
                .then_inc(const_landed, 16)
            for l in range(2):
                for k in range(CONV):
                    sp.dma_start(prow[:, 4 * l + k], ffn_conv_w[l, k].rearrange("(t p) -> t p", p=P)) \
                        .then_inc(const_landed, 16)
                sp.dma_start(prow[:, 4 * l + 3], ffn_conv_b[l].rearrange("(t p) -> t p", p=P)) \
                    .then_inc(const_landed, 16)
            sp.dma_start(ln_rows[:, 0], ln_gain.rearrange("l w (t p) -> (l w t) p", p=P)).then_inc(const_landed, 16)
            sp.dma_start(ln_rows[:, 1], ln_bias.rearrange("l w (t p) -> (l w t) p", p=P)).then_inc(const_landed, 16)
            sp.dma_start(dec, decay).then_inc(const_landed, 16)
            sp.dma_start(tapsw, pool_taps).then_inc(const_landed, 16)
            sp.dma_start(pw[:], pool_w[0].rearrange("g (t p) n -> p g t n", p=P)).then_inc(const_landed, 16)
            sp.dma_start(sink_row[:], attn_sinks.to_broadcast([P, AH])).then_inc(const_landed, 16)
            for s in range(10, S_EVEN_OUT):
                even_in(s)
            for i in range(NCH * KG):
                n, kg = divmod(i, KG)
                kg = EVEN_OUT_KG[kg]
                load(S_EVEN_OUT + i, w_even_out[:, GK * kg:GK * kg + GK, cols(n * COLS)])
                if i == 4:
                    sp.wait_ge(t_ready, FILL_LN0)
                    load_params(0)
            ffn(0)
            for s in range(S_ODD_IN, S_ODD_OUT):
                c, kg = divmod(s - S_ODD_IN, KG)
                load(s, w_qkv[:, GK * kg:GK * kg + GK, cols(ODD_COLS[c])])
                if s == S_ODD_IN + 3:
                    sp.wait_ge(t_ready, FILL_LN1 + 2)
                    sp.dma_start(dist, distance).then_inc(const_landed, 16)
                    sp.dma_start(v_bias, attn_b_qkv[0:1, 18 * P:20 * P].to_broadcast([P, 2 * P])) \
                        .then_inc(const_landed, 16)
            for i, (n, kg) in enumerate(ODD_OUT_ORDER):
                load(S_ODD_OUT + i, w_att_out[:, GK * kg:GK * kg + GK, cols(n * COLS)])
                if i == 12:
                    sp.wait_ge(t_ready, FILL_LN2)
                    load_params(2)
            ffn(1)
            for q in range(2):
                sp.wait_ge(last_first, q + 1)
                sp.dma_start(out_t[:, 0, cols(2 * q * COLS, 2 * COLS)], xres[:, 0, cols(2 * q * COLS, 2 * COLS)]) \
                    .then_inc(stored, 16)
            sp.wait_ge(last_second, 1)
            sp.dma_start(out_t[:, 1, cols((NCH - 1) * COLS)], xres[:, 1, cols((NCH - 1) * COLS)]) \
                .then_inc(stored, 16)
            for n0, n1 in ((0, NCH - 2), (NCH - 2, NCH - 1)):
                c = slice(COLS * n0, COLS * n1)
                sp.wait_ge(last_scaled, n1)
                sp.dma_start(out_t[:, 1, c], xres[:, 1, c]).then_inc(stored, 16)
            sp.wait_ge(stored, 16 * 5)

        @block.gpsimd
        def _(pool):
            nc.gpsimd.memset(ident[:], 0.0).then_inc(ident_ready, 1)
            pool.wait_ge(ident_ready, 1)
            nc.gpsimd.affine_select(out=ident[:], in_=ident[:], compare_op=ALU.not_equal, fill=1.0, base=0,
                                    pattern=[[-1, P]], channel_multiplier=1).then_inc(ident_ready, 1)

            pool.wait_ge(turned, FILL_X + 8)
            for a in range(TOK):
                nc.gpsimd.tensor_scalar(xres[:, a], xres[:, a], ALPHA, 1.0, ALU.mult, ALU.mult) \
                    .then_inc(scaled, 1)
            steps = 0
            for m in range(3):
                pool.wait_ge(lnp_landed, 32 * (m + 1))
                nc.gpsimd.tensor_scalar(lnp, lnp, ALPHA, 1.0, ALU.mult, ALU.mult).then_inc(pool_step, 1)
                pool.wait_ge(turned, FILL_LN[m] + 8)
                steps += 1
                pool.wait_ge(pool_step, steps)
                for a in range(TOK):
                    nc.gpsimd.tensor_tensor(xres[:, a], xres[:, a], lnp[:, 0], ALU.mult).then_inc(pool_step, 1)
                for a in range(TOK):
                    pool.wait_ge(pool_step, steps + a + 1)
                    nc.gpsimd.tensor_tensor(xres[:, a], xres[:, a], lnp[:, 1], ALU.add).then_inc(scaled, 1)
                steps += TOK

            pool.wait_ge(lnp_landed, 32 * 4)
            for n in range(NCH - 1):
                c = slice(COLS * n, COLS * n + COLS)
                pool.wait_ge(last_normed, n + 1)
                nc.gpsimd.tensor_tensor(xres[:, 1, c], xres[:, 1, c], lnp[:, 0, c], ALU.mult).then_inc(pool_step, 1)
                steps += 1
                pool.wait_ge(pool_step, steps)
                nc.gpsimd.tensor_tensor(xres[:, 1, c], xres[:, 1, c], lnp[:, 1, c], ALU.add).then_inc(last_scaled, 1)

        @block.scalar
        def _(act):
            def high(s, turn=0):
                if s >= S_END:
                    return
                act.wait_ge(raw_landed[s % RAW], 16 * (s // RAW + 1) + turn * (16 * (12 // RAW)))
                if not isinstance(turn, int) or s >= HI:
                    act.wait_ge(used, s - HI + 1 + turn * 12)
                nc.scalar.activation(w_hi[:, s % HI], raw[:, s % RAW], ACT.Copy).then_inc(hi_ready, 1)

            def high_first(k):
                if k < GK - 1:
                    act.wait_ge(first_landed[k], 16)
                else:
                    act.wait_ge(raw_landed[0], 16)
                nc.scalar.activation(w_hi[:, 0, k], raw[:, 0, k], ACT.Copy) \
                    .then_inc(first_hi if k < GK - 1 else hi_ready, 1)

            def fill_high(n, j):
                act.wait_ge(turned, n + 1)
                nc.scalar.activation(T[:, 2 * j:2 * j + 2, 0:SEQ],
                                     ps[:, fill_bank(n)].rearrange("p (t n) -> p t n", t=2),
                                     ACT.Copy).then_inc(t_hi, 1)

            def fill_normed(m, s):
                for j in range(8):
                    n = FILL_LN[m] + j
                    act.wait_ge(turned, n + 1)
                    if j >= 2:
                        act.wait_ge(t_ready, n - 1)
                    for t in range(2):
                        c = KT * m + 2 * j + t
                        ins = nc.scalar.activation(half[:, n % 2, t], ps[:, fill_bank(n), SEQ * t:SEQ * t + SEQ],
                                                   ACT.Identity, bias=ln_cols[:, 1, c:c + 1],
                                                   scale=ln_cols[:, 0, c:c + 1])
                    ins.then_inc(act_step, 1)
                    act.wait_ge(act_step, 8 * m + j + 1)
                    nc.scalar.activation(T[:, 2 * j:2 * j + 2, 0:SEQ], half[:, n % 2], ACT.Copy).then_inc(t_hi, 1)
                    if j in SPLIT_AFTER:
                        high(s + HI_LEAD + SPLIT_AFTER[j])

            def halves(n, bank, ended, turn=0):
                act.wait_ge(used, ended + turn * 12)
                if not isinstance(turn, int) or n >= 2:
                    act.wait_ge(added, n - 1 + turn * 4)
                nc.scalar.activation(half[:, n % 2], ps[:, bank:bank + 2, SEQ:2 * SEQ], ACT.Copy) \
                    .then_inc(half_out, 1)

            def ln_root(m):
                act.wait_ge(var_ready, m + 2)
                nc.scalar.activation(rstd[:], rstd[:], ACT.Sqrt).then_inc(std_ready, 1)

            for s in range(KG):
                for j in (2 * s, 2 * s + 1):
                    fill_high(FILL_X + j, j)
                    if s == 0:
                        high_first(2 * j)
                        high_first(2 * j + 1)
                high(s + 1)
            for s in range(1, S_EVEN_OUT):
                c, kg = divmod(s, KG)
                if kg == 0 and 1 <= c <= 4:
                    for q in range(2):
                        halves(2 * (c - 1) + q, 4 * ((c - 1) % 2) + 2 * q, s)
                if kg == 0 and 5 <= c <= 8:
                    act.wait_ge(used, s)
                    to = (v_nat, u_nat)[(c - 5) // 2]
                    lo, b = COLS * ((c - 5) % 2), 2 * ((c - 5) % 2)
                    nc.scalar.activation(to[:, :, lo:lo + COLS], ps[:, b:b + 2], ACT.Copy).then_inc(vug_out, 1)
                if s == 4 * 9:
                    act.wait_ge(used, s)
                    act.wait_ge(ret_mixed, RH)
                    nc.scalar.activation(silu_g[:, :, 0:COLS], ps[:, 0:2], ACT.Silu).then_inc(vug_out, 1)
                if s > 1:
                    high(s + HI_LEAD)
                if s == PARAMS_AT + 1:
                    act.wait_ge(params_turned, 1)
                    for l in range(2):
                        nc.scalar.activation(taps[:, 4 * l:4 * l + 4],
                                             ps[:, 4 + l, 0:4 * FT].rearrange("p (t n) -> p t n", t=4), ACT.Copy) \
                            .then_inc(params_ready, 1)
                    nc.scalar.activation(qk_bias[:], ps[:, 6, 0:18], ACT.Copy).then_inc(params_ready, 1)
                    nc.scalar.activation(p_scale[:], ps[:, 6, 32:40], ACT.Copy).then_inc(params_ready, 1)
                    nc.scalar.activation(ln_cols[:], ps[:, 7, 0:8 * KT].rearrange("p (w n) -> p w n", w=2),
                                         ACT.Copy).then_inc(params_ready, 1)
                hd = s - (RET_AT + 2)
                if 0 <= hd < RH:
                    act.wait_ge(ret_mixed, hd + 1)
                    nc.scalar.activation(y_nat[:, :, RD * hd:RD * hd + RD],
                                         ps[:, mix_bank(hd)].rearrange("p (a n) -> p a n", a=TOK), ACT.Copy) \
                        .then_inc(ret_out, 1)
                if s == RET_AT + 6:
                    act.wait_ge(var_ready, 1)
                    nc.scalar.activation(r_std[:], r_std[:], ACT.Sqrt).then_inc(std_ready, 1)
                i = s - (POOL_AT + 1)
                if 0 <= i < 2:
                    act.wait_ge(pooled, i + 1)
                    for n in (2 * i, 2 * i + 1):
                        nc.scalar.activation(pooledT[:, 2 * n:2 * n + 2],
                                             ps[:, 4 + n].rearrange("p (t n) -> p t n", t=2), ACT.Copy) \
                            .then_inc(pooled_out, 1)
                i = s - (POOL_AT + 3)
                if 0 <= i < 2:
                    act.wait_ge(pool_mixed, i + 1)
                    for n in range(4 * i, 4 * i + 4):
                        nc.scalar.activation(poolT[:, n], ps[:, 4 + n // 2, SEQ * (n % 2):SEQ * (n % 2) + SEQ],
                                             ACT.Copy, scale=p_scale[:, n:n + 1]).then_inc(pool_out, 1)
                if s == POOL_AT + 5:
                    act.wait_ge(pool_out, 4)
                    nc.scalar.activation(gT[:, :, 0:SEQ], poolT[:, 0:4], ACT.Copy).then_inc(pool_hi, 1)

            act.wait_ge(used, S_EVEN_OUT)
            act.wait_ge(pool_out, 8)
            nc.scalar.activation(T[:, 12:16, 0:SEQ], poolT[:, 4:8], ACT.Copy).then_inc(pool_hi, 1)
            nc.scalar.activation(silu_g[:, :, COLS:2 * COLS], ps[:, 2:4], ACT.Silu).then_inc(vug_out, 1)
            for n in range(4):
                fill_high(FILL_RET + n, n)
            for s in range(S_EVEN_OUT, S_FFN0):
                high(s + HI_LEAD)

            def gelu(n, q, turn=0):
                act.wait_ge(conv_done, n + turn * 2)
                nc.scalar.activation(conv_g[:, 2 * q:2 * q + 2], conv_g[:, 2 * q:2 * q + 2], ACT.Gelu) \
                    .then_inc(gelu_out, 1)

            def gated_high(n, q, turn=0, to=gT):
                act.wait_ge(gated_out, n + turn * 2)
                nc.scalar.activation(to[:, 2 * q:2 * q + 2, 0:SEQ], gated[:, 2 * q:2 * q + 2], ACT.Copy) \
                    .then_inc(g_hi, 1)

            def feed_forward(l):
                base, tp, gp = S_FFN[l], TP_FFN[l], 2 * FC * l
                ln_root(2 * l)
                fill_normed(2 * l, base)
                for j in range(1, 8):
                    if j > 2:
                        high(base + j + HI_LEAD)
                    if j == 4:
                        for q in range(2):
                            halves(tp + q, 2 * q, base + 4)
                    if j in (5, 6):
                        gelu(gp + j - 4, j - 5)
                with act.Fori(0, TURNS) as turn:
                    s = base + 2 * KG
                    for j in range(12):
                        high(s + j + HI_LEAD, turn)
                        if j == 0:
                            for q in range(2):
                                halves(tp + 2 + q, 4 + 2 * q, s, turn)
                        if j == 4:
                            for q in range(2):
                                halves(tp + 4 + q, 2 * q, s + 4, turn)
                        if j in (1, 2):
                            gated_high(gp + j, j - 1, turn)
                        if j in (5, 6):
                            gelu(gp + 2 + j - 4, j - 5, turn)
                tail, c = base + FFN_GROUPS - 4 * KG, FC - 1
                for j in range(16):
                    high(tail + j + HI_LEAD)
                    if j in (0, 4, 8):
                        k = j // 4
                        for q in range(2):
                            halves(tp + 4 * c - 2 + 2 * k + q, (4, 0, 4)[k] + 2 * q, tail + j)
                    if j in (1, 2):
                        gated_high(gp + 2 * (c - 1) + j, j - 1)
                    if j in (5, 6):
                        gelu(gp + 2 * c + j - 4, j - 5)
                    if j in (9, 10):
                        gated_high(gp + 2 * c + j - 8, j - 9, to=T)

            feed_forward(0)

            def attention(s):
                b = s - 1 - ATT_AT
                if 0 <= b - 1 < PAIRS:
                    act.wait_ge(att_turned, b)
                    nc.scalar.activation(PT, ps[:, 6:8, 0:3 * P], ACT.Copy).then_inc(att_pt, 1)
                if 0 <= b < PAIRS:
                    act.wait_ge(att_max, b + 1)
                    for a in range(2):
                        for blk, (lo, n) in enumerate(((0, P), (P, 2 * P))):
                            nc.scalar.activation(S[:, a, lo:lo + n], S[:, a, lo:lo + n], ACT.Exp,
                                                 bias=nm[:, b, a, blk:blk + 1],
                                                 accum_out=rs[:, b, a, blk:blk + 1])
                    nc.scalar.activation(es[:, b], es[:, b], ACT.Exp).then_inc(att_exp, 1)

            ln_root(1)
            fill_normed(1, S_ODD_IN)
            for s in range(S_ODD_IN + 1, S_FFN1):
                if s == S_ODD_IN + KG:
                    halves(TP_ODD, 0, s)
                if s == S_ODD_IN + KG + 1:
                    act.wait_ge(akv_ready, 2)
                    act.dma_start(akT[64:128, 0:KVH:2], akT[0:64, 0:KVH:2]).then_inc(key_copied, 16)
                    act.dma_start(akT[0:64, 1:KVH:2], akT[64:128, 1:KVH:2]).then_inc(key_copied, 16)
                cc = (s - S_ODD_IN) // KG - 2
                if (s - S_ODD_IN) % KG == 0 and 0 <= cc < 4:
                    for q in range(2):
                        halves(TP_ODD + 1 + 2 * cc + q, q_bank(cc) + 2 * q, s)
                if s - S_ODD_OUT in ATT_FILL_AT:
                    for t in (0, 1):
                        j = ATT_FILL_AT[s - S_ODD_OUT] + t
                        fill_high(FILL_ATT + j, j)
                attention(s)
                if s > S_ODD_IN + 2:
                    high(s + HI_LEAD)
            feed_forward(1)
            ln_root(3)
            act.wait_ge(shift_ready, 1)
            for n in range(NCH):
                c = slice(COLS * n, COLS * n + COLS)
                nc.scalar.activation(xres[:, 1, c], xres[:, 1, c], ACT.Identity, bias=shift[:], scale=rstd[:, 1:2]) \
                    .then_inc(last_normed, 1)

        @block.vector
        def _(dve):
            own = Count()
            vec = nc.vector

            def chain(ins):
                own.n += 1
                ins.then_inc(dve_step, 1)
                dve.wait_ge(dve_step, own.now())

            def low(s, turn=0):
                if s >= S_END:
                    return
                dve.wait_ge(hi_ready, s + 1 + turn * 12)
                if not isinstance(turn, int) or s >= LO:
                    dve.wait_ge(used, s - LO + 1 + turn * 12)
                vec.tensor_tensor(w_lo[:, s % LO], raw[:, s % RAW], w_hi[:, s % HI].bitcast(F32),
                                  ALU.subtract).then_inc(lo_ready, 1)

            def low_first(k):
                if k < GK - 1:
                    dve.wait_ge(first_hi, k + 1)
                else:
                    dve.wait_ge(hi_ready, 1)
                vec.tensor_tensor(w_lo[:, 0, k], raw[:, 0, k], w_hi[:, 0, k].bitcast(F32), ALU.subtract) \
                    .then_inc(first_lo if k < GK - 1 else lo_ready, 1)

            def fill_low(n, j):
                dve.wait_ge(t_hi, n + 1)
                vec.tensor_tensor(T[:, 2 * j:2 * j + 2, SEQ:2 * SEQ],
                                  ps[:, fill_bank(n)].rearrange("p (t n) -> p t n", t=2),
                                  T[:, 2 * j:2 * j + 2, 0:SEQ].bitcast(F32), ALU.subtract).then_inc(t_ready, 1)

            def pair_sum(to, n, bank, turn=0):
                dve.wait_ge(half_out, n + 1 + turn * 4)
                vec.tensor_tensor(to, ps[:, bank:bank + 2, 0:SEQ], half[:, n % 2], ALU.add).then_inc(added, 1)

            def add_chunk(n, bank, count_in, done=None):
                c = slice(COLS * n, COLS * n + COLS)
                vec.tensor_tensor(xres[:, :, c], xres[:, :, c], ps[:, bank:bank + 2], ALU.add).then_inc(count_in, 1)
                if done is not None:
                    dve.wait_ge(count_in, done)
                    for a in range(TOK):
                        vec.bn_stats(stats[:, a, n], xres[:, a, c])

            def add_last(m, bank, count_in, ended):
                n = NCH - 1
                c = slice(COLS * n, COLS * n + COLS)
                for a in range(TOK):
                    if a == 0:
                        dve.wait_ge(last_half, m + 1)
                    else:
                        dve.wait_ge(used, ended)
                    ins = vec.tensor_tensor(xres[:, a, c], xres[:, a, c], ps[:, bank + a], ALU.add)
                    if a == TOK - 1:
                        ins.then_inc(count_in[0], 1)
                        dve.wait_ge(*count_in)
                    else:
                        chain(ins)
                    ins = vec.bn_stats(stats[:, a, n], xres[:, a, c])
                chain(ins)

            def inverse_root(m):
                for a in range(TOK):
                    ins = vec.bn_aggr(mean_var[:, a], stats[:, a])
                chain(ins)
                vec.tensor_scalar(rstd[:], mean_var[:, :, 1], EPS, None, ALU.add).then_inc(var_ready, 1)
                dve.wait_ge(std_ready, m + 2)
                chain(vec.reciprocal(rstd[:], rstd[:]))

            def fill_normed_low(n, j):
                dve.wait_ge(t_hi, n + 1)
                vec.tensor_tensor(T[:, 2 * j:2 * j + 2, SEQ:2 * SEQ], half[:, n % 2],
                                  T[:, 2 * j:2 * j + 2, 0:SEQ].bitcast(F32), ALU.subtract).then_inc(t_ready, 1)

            def layer_norm(m, s):
                inverse_root(m)

                def normalise(q):
                    for a in range(TOK):
                        c = slice(COLS * q, COLS * q + COLS)
                        ins = vec.tensor_scalar(xres[:, a, c], xres[:, a, c], mean_var[:, a, 0:1],
                                                rstd[:, a:a + 1], ALU.subtract, ALU.mult)
                    ins.then_inc(ln_chunk, 1)

                for q in range(3):
                    normalise(q)
                for j in range(8):
                    fill_normed_low(FILL_LN[m] + j, j)
                    if j == 0:
                        normalise(3)
                    if j == 1 and m == 1:
                        low(s + LO_LEAD - 1)
                    if j in SPLIT_AFTER:
                        low(s + LO_LEAD + SPLIT_AFTER[j])

            def last_layer_norm():
                m = 3
                inverse_root(m)
                vec.scalar_tensor_tensor(shift[:], mean_var[:, 1, 0:1], -1.0, rstd[:, 1:2], ALU.mult, ALU.mult) \
                    .then_inc(shift_ready, 1)
                dve.wait_ge(lnp_landed, 32 * (m + 1))
                for q in range(0, NCH, 2):
                    cs = [slice(COLS * n, COLS * n + COLS) for n in (q, q + 1)]
                    for c in cs:
                        ins = vec.scalar_tensor_tensor(xres[:, 0, c], xres[:, 0, c], mean_var[:, 0, 0:1],
                                                       lnp[:, 0, c], ALU.subtract, ALU.mult)
                    chain(ins)
                    for c in cs:
                        ins = vec.scalar_tensor_tensor(xres[:, 0, c], xres[:, 0, c], rstd[:, 0:1],
                                                       lnp[:, 1, c], ALU.mult, ALU.add)
                    ins.then_inc(last_first, 1)
                c = slice(COLS * (NCH - 1), COLS * NCH)
                dve.wait_ge(last_normed, NCH)
                chain(vec.tensor_tensor(xres[:, 1, c], xres[:, 1, c], lnp[:, 0, c], ALU.mult))
                vec.tensor_tensor(xres[:, 1, c], xres[:, 1, c], lnp[:, 1, c], ALU.add).then_inc(last_second, 1)

            for s in range(KG):
                for j in (2 * s, 2 * s + 1):
                    fill_low(FILL_X + j, j)
                    if s == 0:
                        low_first(2 * j)
                        low_first(2 * j + 1)
                low(s + 1)
            for s in range(1, S_EVEN_OUT):
                c, kg = divmod(s, KG)
                if kg == 0 and 1 <= c <= 4:
                    for q in range(2):
                        to = (qT, kT)[(c - 1) // 2]
                        t = TPC * ((c - 1) % 2) + 2 * q
                        pair_sum(to[:, t:t + 2], 2 * (c - 1) + q, 4 * ((c - 1) % 2) + 2 * q)
                hd = s - (RET_AT + 1)
                if 0 <= hd < RH:
                    dve.wait_ge(ret_scored, hd + 1)
                    if hd == 0:
                        dve.wait_ge(const_landed, CONSTS)
                    vec.tensor_tensor(probs[:, hd % 2], ps[:, ret_bank(hd), 0:3 * P], dec[:, hd], ALU.mult) \
                        .then_inc(ret_probs, 1)
                if s > 2:
                    low(s + LO_LEAD)
                hd = s - (RET_AT + 2)
                if 0 <= hd < RH:
                    dve.wait_ge(ret_out, hd + 1)
                    for a in range(TOK):
                        ins = vec.bn_stats(r_stats[:, TOK * hd + a], y_nat[:, a, RD * hd:RD * hd + RD])
                    if hd == RH - 1:
                        chain(ins)
                        for i in range(TOK * RH):
                            ins = vec.bn_aggr(r_mv[:, i], r_stats[:, i])
                        chain(ins)
                        vec.tensor_scalar(r_std[:], r_mv[:, :, 1:2], EPS, None, ALU.add).then_inc(var_ready, 1)
                if s == RET_AT + 7:
                    dve.wait_ge(std_ready, 1)
                    chain(vec.reciprocal(r_std[:], r_std[:]))
                    for hd in range(RH):
                        for a in range(TOK):
                            i = TOK * hd + a
                            yy = y_nat[:, a, RD * hd:RD * hd + RD]
                            ins = vec.tensor_scalar(yy, yy, r_mv[:, i, 0:1], r_std[:, i], ALU.subtract, ALU.mult)
                    chain(ins)
                if s == 4 * 9:
                    dve.wait_ge(vug_out, 5)
                    vec.tensor_tensor(y_nat[:, :, 0:COLS], y_nat[:, :, 0:COLS], silu_g[:, :, 0:COLS], ALU.mult) \
                        .then_inc(ret_gated, 1)
                    for blk in range(2):
                        vec.tensor_scalar(neg_sink[:, :, blk], sink_row[:], -1.0, None, ALU.mult)
                if s == POOL_AT + 6:
                    dve.wait_ge(pool_hi, 1)
                    vec.tensor_tensor(gT[:, :, SEQ:2 * SEQ], poolT[:, 0:4], gT[:, :, 0:SEQ].bitcast(F32),
                                      ALU.subtract).then_inc(pool_ready, 1)
            dve.wait_ge(pool_hi, 2)
            vec.tensor_tensor(T[:, 12:16, SEQ:2 * SEQ], poolT[:, 4:8], T[:, 12:16, 0:SEQ].bitcast(F32),
                              ALU.subtract).then_inc(pool_ready, 1)
            dve.wait_ge(vug_out, 6)
            vec.tensor_tensor(y_nat[:, :, COLS:RW], y_nat[:, :, COLS:RW], silu_g[:, :, COLS:RW], ALU.mult) \
                .then_inc(ret_gated, 1)
            for n in range(4):
                fill_low(FILL_RET + n, n)
            for s in range(S_EVEN_OUT, S_FFN0):
                i = s - S_EVEN_OUT
                if i % KG == 0 and i:
                    n = i // KG - 1
                    dve.wait_ge(used, s)
                    dve.wait_ge(scaled, TOK)
                    add_chunk(n, 2 * (n % 2), proj_added, n + 1)
                low(s + LO_LEAD)
            add_last(0, 2, (proj_added, NCH), S_FFN0)

            def convolve(kind, q, conv, cur, bank, n, turn=0, count_in=None):
                t = 2 * q
                pair_sum(h[:, t:t + 2, CONV - 1:], n, bank, turn)
                dve.wait_ge(added, n + 1 + turn * 4)
                for k in range(CONV):
                    for i in (t, t + 1):
                        if k == 0:
                            ins = vec.tensor_scalar(conv[:, i], h[:, i, 0:SEQ], cur[:, kind, 0, i:i + 1],
                                                    cur[:, kind, 3, i:i + 1], ALU.mult, ALU.add)
                        else:
                            ins = vec.scalar_tensor_tensor(conv[:, i], h[:, i, k:k + SEQ],
                                                           cur[:, kind, k, i:i + 1], conv[:, i],
                                                           ALU.mult, ALU.add)
                    if k < CONV - 1 or kind == 1:
                        chain(ins)
                    else:
                        ins.then_inc(conv_done, 1)

            def feed_forward(l):
                base, tp, gp = S_FFN[l], TP_FFN[l], 2 * FC * l
                outs = NCH * FC * l
                layer_norm(2 * l, base)
                chain(vec.memset(h[:, :, 0:CONV - 1], 0.0))

                def current(kind, first):
                    chain(vec.tensor_copy(cur[:, kind], taps[:, 4 * l:4 * l + 4, first]))

                def value_pair(q, n, g, turn=0):
                    convolve(1, q, conv_v, cur, 4 + 2 * q, n, turn)
                    dve.wait_ge(gelu_out, g + turn * 2)
                    vec.tensor_tensor(gated[:, 2 * q:2 * q + 2], conv_v[:, 2 * q:2 * q + 2],
                                      conv_g[:, 2 * q:2 * q + 2], ALU.mult).then_inc(gated_out, 1)

                def gated_low(q, g, turn=0, to=gT):
                    dve.wait_ge(g_hi, g + turn * 2)
                    vec.tensor_tensor(to[:, 2 * q:2 * q + 2, SEQ:2 * SEQ], gated[:, 2 * q:2 * q + 2],
                                      to[:, 2 * q:2 * q + 2, 0:SEQ].bitcast(F32), ALU.subtract) \
                        .then_inc(g_ready, 1)

                for j in range(1, 8):
                    if j > 2:
                        low(base + j + LO_LEAD)
                    if j == 4:
                        current(0, slice(0, TPC))
                    if j in (4, 5):
                        convolve(0, j - 4, conv_g, cur, 2 * (j - 4), tp + j - 4)
                with dve.Fori(0, TURNS) as turn:
                    own.enter(turn, LOOP_OWN)
                    s = base + 2 * KG
                    for j in range(12):
                        if j == 8:
                            dve.wait_ge(used, s + 8 + turn * 12)
                            add_chunk(3, 6, ffn_added)
                        if j in (5, 6, 7):
                            dve.wait_ge(used, s + j + turn * 12)
                            if j == 5:
                                dve.wait_ge(scaled, TOK * (2 + 2 * l))
                            add_chunk(j - 5, 4 + 2 * ((j - 5) % 2), ffn_added)
                        low(s + j + LO_LEAD, turn)
                        if j == 0:
                            current(1, bass.ds(FT // 2 + turn * TPC, TPC))
                        if j in (0, 1):
                            value_pair(j, tp + 2 + j, gp + 1 + j, turn)
                        if j in (2, 3):
                            gated_low(j - 2, gp + j - 1, turn)
                        if j == 4:
                            current(0, bass.ds((turn + 1) * TPC, TPC))
                        if j in (4, 5):
                            convolve(0, j - 4, conv_g, cur, 2 * (j - 4), tp + j, turn)
                    own.leave(TURNS)
                tail, c = base + FFN_GROUPS - 4 * KG, FC - 1
                for j in range(16):
                    if j == 11:
                        gated_low(1, gp + 2 * c + 2, to=T)
                    if j in (9, 10, 12):
                        dve.wait_ge(used, tail + j)
                        add_chunk(j - 9, 2 * ((j - 9) % 2), ffn_added)
                    if 13 <= j:
                        n = j - 13
                        dve.wait_ge(used, tail + j)
                        add_chunk(n, 4 + 2 * (n % 2), ffn_added, outs + NCH * c + n + 1)
                    if j < 15:
                        low(tail + j + LO_LEAD)
                    if j == 0:
                        current(1, slice(FT // 2 + TPC * (c - 1), FT // 2 + TPC * c))
                    if j in (0, 1):
                        value_pair(j, tp + 4 * c - 2 + j, gp + 2 * c - 1 + j)
                    if j in (2, 3):
                        gated_low(j - 2, gp + 2 * c - 1 + j - 2)
                    if j == 4:
                        current(0, slice(TPC * c, TPC * c + TPC))
                    if j in (4, 5):
                        convolve(0, j - 4, conv_g, cur, 2 * (j - 4), tp + 4 * c + j - 4)
                    if j == 8:
                        current(1, slice(FT - TPC, FT))
                    if j in (8, 9):
                        value_pair(j - 8, tp + 4 * c + 2 + j - 8, gp + 2 * c + 1 + j - 8)
                    if j == 10:
                        gated_low(0, gp + 2 * c + 1, to=T)
                    if j == 11:
                        dve.wait_ge(used, tail + j)
                        add_chunk(2, 0, ffn_added)
                add_last(2 * l + 1, 6, (ffn_added, outs + NCH * FC), tail + 16)

            feed_forward(0)

            def attention_max(s):
                b = s - 1 - ATT_AT
                if not 0 <= b < PAIRS:
                    return
                dve.wait_ge(att_scored, b + 1)
                for a in range(2):
                    slope = 2.0 ** (-8.0 / AH * (2 * b + a + 1))
                    ins = vec.scalar_tensor_tensor(S[:, a], dist, slope, ps[:, 4 + a, 0:3 * P],
                                                   ALU.mult, ALU.add)
                ins.then_inc(att_biased, 1)
                dve.wait_ge(att_biased, b + 1)
                vec.tensor_reduce(m_pair[:, b, :, 0], S[:, :, 0:P], AX_X, ALU.max)
                chain(vec.tensor_reduce(m_pair[:, b, :, 1], S[:, :, P:3 * P], AX_X, ALU.max))
                chain(vec.scalar_tensor_tensor(nm[:, b], m_pair[:, b], -1.0, neg_sink[:, 2 * b:2 * b + 2],
                                               ALU.mult, ALU.min))
                vec.tensor_tensor(es[:, b], nm[:, b], neg_sink[:, 2 * b:2 * b + 2], ALU.subtract) \
                    .then_inc(att_max, 1)

            def attention_out(s):
                b = s - 1 - ATT_AT
                if 0 <= b - 1 < PAIRS:
                    dve.wait_ge(att_exp, b)
                    chain(vec.tensor_tensor(es[:, b - 1], rs[:, b - 1], es[:, b - 1], ALU.add))
                    chain(vec.reciprocal(rinv[:, b - 1], es[:, b - 1]))
                if 0 <= b - 2 < PAIRS:
                    p = b - 2
                    dve.wait_ge(att_mixed, p + 1)
                    if b - 1 < PAIRS:
                        dve.wait_ge(att_pt, b)
                    for a in range(2):
                        o = AD * (2 * p + a)
                        ins = vec.tensor_tensor(o_nat[:, :, o:o + AD],
                                                ps[:, 6 + a, 3 * P:4 * P].rearrange("p (b n) -> p b n", b=2),
                                                rinv[:, p, a].unsqueeze(2).to_broadcast([P, 2, AD]), ALU.mult)
                    ins.then_inc(att_out, 1)

            layer_norm(1, S_ODD_IN)
            for s in range(S_ODD_IN + 1, S_FFN1):
                cc = (s - S_ODD_IN) // KG - 2
                if s == S_ODD_IN + KG:
                    dve.wait_ge(half_out, TP_ODD + 1)
                    for t in range(2):
                        for hf in range(2):
                            r = slice(64 * hf, 64 * hf + 64)
                            ins = vec.scalar_tensor_tensor(akT[r, 2 * t + hf], ps[r, t, 0:SEQ],
                                                           qk_bias[r, 16 + t:17 + t], half[r, TP_ODD % 2, t],
                                                           ALU.add, ALU.add)
                    ins.then_inc(added, 1)
                    dve.wait_ge(added, TP_ODD + 1)
                    for hf in range(2):
                        r = slice(64 * hf, 64 * hf + 64)
                        vec.tensor_scalar(akT[r, hf:KVH:2], akT[r, hf:KVH:2], AD ** -0.5, None, ALU.mult) \
                            .then_inc(akv_ready, 1)
                    dve.wait_ge(const_landed, CONSTS + 32)
                    for a in range(TOK):
                        ins = vec.tensor_tensor(av[:, a], ps[:, 2 + a, 0:SEQ], v_bias, ALU.add)
                    ins.then_inc(akv_ready, 1)
                if (s - S_ODD_IN) % KG == 0 and 0 <= cc < 4:
                    if cc == 0:
                        dve.wait_ge(scaled, TOK * 3)
                    for q in range(2):
                        n = TP_ODD + 1 + 2 * cc + q
                        dve.wait_ge(half_out, n + 1)
                        for i in range(2):
                            t = TPC * cc + 2 * q + i
                            ins = vec.scalar_tensor_tensor(aqT[:, t], ps[:, q_bank(cc) + 2 * q + i, 0:SEQ],
                                                           qk_bias[:, t:t + 1], half[:, n % 2, i],
                                                           ALU.add, ALU.add)
                        ins.then_inc(added, 1)
                if s - S_ODD_OUT in ATT_FILL_AT and s != S_ODD_OUT + 6:
                    for t in (0, 1):
                        j = ATT_FILL_AT[s - S_ODD_OUT] + t
                        fill_low(FILL_ATT + j, j)
                i = s - S_ODD_OUT
                if i in ODD_OUT_ENDS:
                    n = ODD_OUT_ENDS[i]
                    dve.wait_ge(used, s)
                    add_chunk(n, ODD_OUT_BANKS[n], proj_added, NCH + n + 1)
                attention_out(s)
                attention_max(s)
                if i == 6:
                    fill_low(FILL_ATT + i, i)
                    fill_low(FILL_ATT + i + 1, i + 1)
                if s > S_ODD_IN + 2:
                    low(s + LO_LEAD)
            add_last(2, ODD_OUT_BANKS[-1], (proj_added, 2 * NCH), S_FFN1)
            feed_forward(1)
            last_layer_norm()

        @block.tensor
        def _(pe):
            mm = nc.tensor.matmul

            def ready(s, turn=0):
                pe.wait_ge(lo_ready, s + 1 + turn * 12)

            def turned_mm(s, kg, k, bank, j):
                t = GK * kg + k
                c = slice(P * j, P * j + P)
                mm(ps[:, bank], w_hi[:, s % HI, k, c], T[:, t], start=kg == 0 and k == 0, stop=False)
                return mm(ps[:, bank, 0:SEQ], w_lo[:, s % LO, k, c], T[:, t, 0:SEQ], start=False,
                          stop=kg == KG - 1 and k == GK - 1)

            def turned_tile(s, kg, bank, j):
                for k in range(GK):
                    ins = turned_mm(s, kg, k, bank, j)
                return ins

            def plain_tile(s, src, first_tile, bank, a, start, stop, c=slice(0, COLS), only=None):
                n = c.stop - c.start
                for k in range(GK) if only is None else (only,):
                    t = first_tile + k
                    x_hi = src[:, t, P * a:P * a + P]
                    x_lo = src[:, t, SEQ + P * a:SEQ + P * a + P]
                    mm(ps[:, bank, 0:n], x_hi, w_hi[:, s % HI, k, c], start=start and k == 0, stop=False)
                    mm(ps[:, bank, 0:n], x_hi, w_lo[:, s % LO, k, c], start=False, stop=False)
                    ins = mm(ps[:, bank, 0:n], x_lo, w_hi[:, s % HI, k, c], start=False,
                             stop=stop and k == GK - 1)
                return ins

            def turn_pair(n, j, source):
                b = fill_bank(n)
                for t in range(2):
                    for a in range(TOK):
                        c = P * (2 * j + t)
                        ins = nc.tensor.transpose(ps[:, b, SEQ * t + P * a:SEQ * t + P * a + P],
                                                  source[:, a, c:c + P], ident[:])
                ins.then_inc(turned, 1)

            def turn_quarter(first, q, m):
                if m is None:
                    pe.wait_ge(x_landed[q], 16)
                else:
                    pe.wait_ge(ln_chunk, NCH * m + q + 1)
                if q >= 2 or m is not None:
                    pe.wait_ge(t_ready, first + 2 * q - 2)
                for j in (2 * q, 2 * q + 1):
                    turn_pair(first + j, j, xres)

            def first_chunk(s0, first, m, product):
                turn_quarter(first, 0, m)
                for kg in range(KG):
                    for part in range(2):
                        pe.wait_ge(t_ready, first + 2 * kg + part + 1)
                        if part == 0 and s0 + kg > 0:
                            ready(s0 + kg)
                        elif part == 1 and kg < KG - 1:
                            turn_quarter(first, kg + 1, m)
                            pe.wait_ge(t_ready, first + 2 * kg + part + 1)
                        for k in (2 * part, 2 * part + 1):
                            if s0 + kg == 0:
                                pe.wait_ge(first_lo, k + 1) if k < GK - 1 else ready(0)
                            ins = product(s0 + kg, kg, k)
                    ins.then_inc(used, 1)

            def turned_step(s, kg, k, tiles=TPC):
                for j in range(tiles):
                    ins = turned_mm(s, kg, k, j, j)
                return ins

            pe.wait_ge(ident_ready, 2)
            first_chunk(0, FILL_X, None, turned_step)
            for s in range(KG, S_EVEN_OUT):
                c, kg = divmod(s, KG)
                if kg == 0:
                    if c == 1:
                        pe.wait_ge(t_ready, FILL_X + 8)
                    elif c <= 5:
                        pe.wait_ge(added, 2 * min(c - 1, 3))
                    elif c <= 9:
                        pe.wait_ge(vug_out, c - 5)
                ready(s)
                if c < 4:
                    for j in range(TPC):
                        ins = turned_tile(s, kg, 4 * (c % 2) + j, j)
                else:
                    for a in range(TOK):
                        ins = plain_tile(s, T, GK * kg, 2 * (c % 2) + a, a, kg == 0, kg == KG - 1)
                ins.then_inc(used, 1)

                if s == PARAMS_AT:
                    pe.wait_ge(const_landed, CONSTS)
                    pe.wait_ge(added, 8)
                    for i in range(8):
                        nc.tensor.transpose(ps[:, 4 + i // 4, FT * (i % 4):FT * (i % 4) + FT], prow[:, i],
                                            ident[0:FT, 0:FT])
                    nc.tensor.transpose(ps[:, 6, 0:18], prow2[:, 0], ident[0:18, 0:18])
                    nc.tensor.transpose(ps[:, 6, 32:40], prow2[0:8, 1], ident[0:8, 0:8])
                    for i in range(2):
                        ins = nc.tensor.transpose(ps[:, 7, 4 * KT * i:4 * KT * i + 4 * KT], ln_rows[:, i],
                                                  ident[0:4 * KT, 0:4 * KT])
                    ins.then_inc(params_turned, 1)
                hd = s - (RET_AT + 1)
                if 0 <= hd < RH:
                    pe.wait_ge(ret_probs, hd + 1)
                    pe.wait_ge(vug_out, 2)
                    if hd >= 2:
                        pe.wait_ge(ret_out, hd - 1)
                    b, v = mix_bank(hd), slice(RD * hd, RD * hd + RD)
                    mm(ps[:, b, 0:RD], probs[:, hd % 2, 0:P], v_nat[:, 0, v], start=True, stop=True)
                    mm(ps[:, b, RD:2 * RD], probs[:, hd % 2, P:2 * P], v_nat[:, 0, v], start=True, stop=False)
                    mm(ps[:, b, RD:2 * RD], probs[:, hd % 2, 2 * P:3 * P], v_nat[:, 1, v], start=False,
                       stop=True).then_inc(ret_mixed, 1)
                hd = s - RET_AT
                if 0 <= hd < RH:
                    pe.wait_ge(params_ready, 5)
                    if hd >= 2:
                        pe.wait_ge(ret_probs, hd - 1)
                    b = ret_bank(hd)
                    for d in range(2):
                        mm(ps[:, b, 0:SEQ], kT[:, 2 * hd + d, 0:P], qT[:, 2 * hd + d], start=d == 0, stop=d == 1)
                    for d in range(2):
                        ins = mm(ps[:, b, SEQ:SEQ + P], kT[:, 2 * hd + d, P:SEQ], qT[:, 2 * hd + d, P:SEQ],
                                 start=d == 0, stop=d == 1)
                    ins.then_inc(ret_scored, 1)
                i = s - POOL_AT
                if 0 <= i < 2:
                    pe.wait_ge(vug_out, 4)
                    pe.wait_ge(ret_out, RH)
                    for n in range(4 * i, 4 * i + 4):
                        b, lo = 4 + n // 2, SEQ * (n % 2)
                        mm(ps[:, b, lo:lo + SEQ], u_nat[:, 0, P * n:P * n + P], tapsw[:, n // 2, 0:SEQ],
                           start=True, stop=False)
                        ins = mm(ps[:, b, lo + P:lo + SEQ], u_nat[:, 1, P * n:P * n + P],
                                 tapsw[:, n // 2, SEQ:SEQ + P], start=False, stop=True)
                    ins.then_inc(pooled, 1)
                i = s - (POOL_AT + 2)
                if 0 <= i < 2:
                    pe.wait_ge(pooled_out, 2 * i + 2)
                    for n in range(4 * i, 4 * i + 4):
                        b, lo = 4 + n // 2, SEQ * (n % 2)
                        for k in range(2):
                            ins = mm(ps[:, b, lo:lo + SEQ], pw[:, n // 2, k, P * (n % 2):P * (n % 2) + P],
                                     pooledT[:, 2 * (n // 2) + k], start=k == 0, stop=k == 1)
                    ins.then_inc(pool_mixed, 1)
                if s == S_EVEN_OUT - 2:
                    pe.wait_ge(pool_out, 8)
                    pe.wait_ge(ret_gated, 1)
                    for j in range(2):
                        turn_pair(FILL_RET + j, j, y_nat)

            def projection(s, n, kg, bank, first, last, in_g=False):
                for a in range(TOK):
                    ins = plain_tile(s, gT if in_g else T, 0 if in_g else GK * kg, bank + a, a, first, last)
                    if a == 0 and last and n == NCH - 1:
                        ins.then_inc(last_half, 1)
                ins.then_inc(used, 1)

            for i in range(NCH * KG):
                s, n, pos = S_EVEN_OUT + i, i // KG, i % KG
                kg = EVEN_OUT_KG[pos]
                if pos == 0:
                    if n < 2:
                        pe.wait_ge(vug_out, 5 + n)
                    else:
                        pe.wait_ge(proj_added, n - 1)
                if n == 0:
                    if pos < 2:
                        pe.wait_ge(pool_ready, pos + 1)
                    else:
                        pe.wait_ge(t_ready, FILL_RET + 2 * (pos - 1))
                ready(s)
                projection(s, n, kg, 2 * (n % 2), pos == 0, pos == KG - 1, in_g=pos == 0)
                if i == 0:
                    pe.wait_ge(ret_gated, 2)
                    for j in (2, 3):
                        turn_pair(FILL_RET + j, j, y_nat)

            def feed_forward(l):
                base, tp, gp, outs = S_FFN[l], TP_FFN[l], 2 * FC * l, NCH * FC * l
                first = FILL_LN[2 * l]
                first_chunk(base, first, 2 * l, turned_step)
                pe.wait_ge(t_ready, first + 8)

                def hidden(s, bank, turn=0, waits=()):
                    for kg in range(KG):
                        ready(s + kg, turn)
                        for j in range(TPC):
                            if kg == 0 and waits and j % 2 == 0:
                                pe.wait_ge(*waits[j // 2])
                            ins = turned_tile(s + kg, kg, bank + j, j)
                        ins.then_inc(used, 1)

                def output(s, c4, c2, turn=0, bank=4, freed=3, src=gT, end=False):
                    pe.wait_ge(g_ready, gp + 2 + c2)
                    for n in range(NCH):
                        if n < 2:
                            pe.wait_ge(added, tp + freed + n + c4)
                        else:
                            pe.wait_ge(ffn_added, outs + n - 1 + c4)
                        ready(s + n, turn)
                        b = bank + 2 * (n % 2)
                        for a in range(TOK):
                            ins = plain_tile(s + n, src, 0, b + a, a, True, True)
                            if end and a == 0 and n == NCH - 1:
                                ins.then_inc(last_half, 1)
                        ins.then_inc(used, 1)

                hidden(base + KG, 4)
                with pe.Fori(0, TURNS) as turn:
                    s = base + 2 * KG
                    pe.wait_ge(added, tp + 2 + turn * 4)
                    hidden(s, 0, turn)
                    output(s + KG, turn * 4, turn * 2, turn)
                    hidden(s + 2 * KG, 4, turn, ((ffn_added, outs + 3 + turn * 4), (ffn_added, outs + 4 + turn * 4)))
                tail, c = base + FFN_GROUPS - 4 * KG, FC - 1
                pe.wait_ge(added, tp + 4 * c - 2)
                hidden(tail, 0)
                hidden(tail + KG, 4, 0, ((added, tp + 4 * c - 1), (added, tp + 4 * c)))
                output(tail + 2 * KG, 4 * (c - 1), 2 * (c - 1), bank=0, freed=5)
                output(tail + 3 * KG, 4 * c, 2 * c, src=T, end=True)

            feed_forward(0)

            def kv_step(s, kg, k):
                turned_step(s, kg, k, 2)
                for a in range(TOK):
                    ins = plain_tile(s, T, GK * kg, 2 + a, a, kg == 0, kg == KG - 1, slice(2 * P, 4 * P), only=k)
                return ins

            def burst(b):
                values_and_transposes(b)
                scores(b)

            def values_and_transposes(b):
                if 0 <= b - 2 < PAIRS:
                    p = b - 2
                    pe.wait_ge(att_pt, p + 1)
                    if p >= 1:
                        pe.wait_ge(att_out, p)
                    for a in range(2):
                        lo, kv = 3 * P, slice(AD * (p // 4), AD * (p // 4) + AD)
                        mm(ps[:, 6 + a, lo:lo + AD], PT[:, a, 0:P], av[:, 0, kv], start=True, stop=True)
                        mm(ps[:, 6 + a, lo + AD:lo + 2 * AD], PT[:, a, P:2 * P], av[:, 0, kv],
                           start=True, stop=False)
                        ins = mm(ps[:, 6 + a, lo + AD:lo + 2 * AD], PT[:, a, 2 * P:3 * P], av[:, 1, kv],
                                 start=False, stop=True)
                    ins.then_inc(att_mixed, 1)
                if 0 <= b - 1 < PAIRS:
                    pe.wait_ge(att_exp, b)
                    for a in range(2):
                        for i in range(3):
                            ins = nc.tensor.transpose(ps[:, 6 + a, P * i:P * i + P], S[:, a, P * i:P * i + P],
                                                      ident[:])
                    ins.then_inc(att_turned, 1)

            def scores(b):
                if b < PAIRS:
                    pe.wait_ge(added, TP_ODD + 1 + 2 * (b // 4 + 1))
                    if b == 0:
                        pe.wait_ge(akv_ready, 3)
                        pe.wait_ge(key_copied, 32)
                    else:
                        pe.wait_ge(att_biased, b)
                    for q, to, k in ((slice(0, P), slice(0, P), slice(0, P)),
                                     (slice(P, SEQ), slice(P, 3 * P), slice(0, SEQ))):
                        for a in range(2):
                            r = slice(64 * a, 64 * a + 64)
                            ins = mm(ps[:, 4 + a, to], aqT[r, b, q], akT[r, b // 4, k], start=True, stop=True)
                    ins.then_inc(att_scored, 1)

            def turn_output(j):
                pe.wait_ge(att_out, 2 * j + 2)
                turn_pair(FILL_ATT + j, j, o_nat)

            first_chunk(S_ODD_IN, FILL_LN1, 1, kv_step)
            pe.wait_ge(t_ready, FILL_LN1 + 8)
            for s in range(S_ODD_IN + KG, S_ODD_OUT):
                c, kg = divmod(s - S_ODD_IN - KG, KG)
                ready(s)
                for j in range(TPC):
                    if kg == 0 and j % 2 == 0:
                        if c == 1:
                            pe.wait_ge(added, TP_ODD + 1) if j == 0 else pe.wait_ge(akv_ready, 3)
                        elif c >= 2:
                            pe.wait_ge(added, TP_ODD + 1 + 2 * (c - 1) + 1 + j // 2)
                    ins = turned_tile(s, kg, q_bank(c) + j, j)
                ins.then_inc(used, 1)
                if ATT_AT <= s < S_ODD_OUT - 1:
                    burst(s - ATT_AT)
            values_and_transposes(S_ODD_OUT - 1 - ATT_AT)
            pe.wait_ge(added, TP_ODD + 9)
            turn_output(0)
            turn_output(1)
            scores(S_ODD_OUT - 1 - ATT_AT)

            for i, (n, kg) in enumerate(ODD_OUT_ORDER):
                s = S_ODD_OUT + i
                b = s - ATT_AT
                if kg == 0 and n == 3:
                    pe.wait_ge(proj_added, NCH + 1)
                if n < 2 and ODD_OUT_ORDER.index((0, kg)) == i:
                    pe.wait_ge(t_ready, FILL_ATT + 2 * kg + 2)
                ready(s)
                projection(s, n, kg, ODD_OUT_BANKS[n], kg == 0, kg == KG - 1)
                if i == 0:
                    turn_output(2)
                    turn_output(3)
                if i == 3:
                    pe.wait_ge(att_biased, PAIRS - 1)
                    turn_output(4)
                    turn_output(5)
                if i == 5:
                    pe.wait_ge(att_biased, PAIRS)
                    turn_output(6)
                if b < BURSTS:
                    values_and_transposes(b)
                if i == 3:
                    pe.wait_ge(t_ready, FILL_ATT + 6)
                if i == 5:
                    turn_output(7)
                scores(b)
            feed_forward(1)


_INS = ["x", "ln_gain", "ln_bias", "even_w_in", "pool_w", "pool_scale", "even_w_out", "attn_w_qkv", "attn_b_qkv",
        "attn_sinks", "attn_w_out", "ffn_w_in", "ffn_conv_w", "ffn_conv_b", "ffn_w_out"]


def shape_tables():
    s, t = np.arange(P)[:, None], np.arange(SEQ)[None, :]
    log_gamma = np.log1p(-(2.0 ** (-5.0 - np.arange(RH))))
    lag = (t - s)[None]
    full = np.where(lag >= 0, np.exp(log_gamma[:, None, None] * np.maximum(lag, 0)), 0.0) * RD ** -0.5
    decay = np.concatenate([full, full[:, :, :P]], axis=2).transpose(1, 0, 2)
    w = np.array(WINDOWS)[:, None, None]
    inside = (lag >= 0) & (lag < w)
    mean = inside / np.minimum(t + 1, w) - (lag == 0)
    later = (inside / w - (lag == 0))[:, :, :P]
    taps = np.concatenate([mean, later], axis=2).transpose(1, 0, 2)
    i, j = np.arange(P)[:, None], np.arange(P)[None, :]
    own_block = np.where(j <= i, j - i, MASKED)
    before = np.where(j > i, j - i - P, MASKED)
    dist = np.concatenate([own_block, before, own_block], axis=1)
    return {n: np.ascontiguousarray(a, dtype=np.float32)
            for n, a in (("decay", decay), ("pool_taps", taps), ("distance", dist))}


def kernel(**inputs):
    import concourse.bacc as bacc
    from concourse.bass_utils import run_bass_kernel_spmd

    nc = bacc.Bacc("TRN2", target_bir_lowering=False, num_devices=1, dynamic_dma_scratch_size=1024)
    arrays, args = {}, []
    for name in _INS:
        a = np.ascontiguousarray(inputs[name])
        arrays[name] = a
        args.append(nc.dram_tensor(name, a.shape, mybir.dt.from_np(a.dtype), kind="ExternalInput").ap())
    for name, a in shape_tables().items():
        arrays[name] = a
        args.append(nc.dram_tensor(name, a.shape, F32, kind="ExternalInput").ap())
    args.append(nc.dram_tensor("out", (1, SEQ, D), F32, kind="ExternalOutput").ap())
    build_trunk(nc, *args)
    r = run_bass_kernel_spmd(nc, [arrays], core_ids=[0])
    return r.results[0]["out"]
```
